# Optimizing a Trainium2 kernel written in Bass

```python
import jax, jax.numpy as jnp
from jax import lax
import numpy as np

D_MODEL = 2048
BATCH = 1
SEQ = 256
DEPTH = 1
DEC_BATCH = 8
DEC_SEQ = 1
PAST_LEN = 2048
PAGE_SIZE = 128

HEAD_DIM = 128
N_HEADS = D_MODEL // HEAD_DIM
H_SB = N_HEADS // 2
H_FOX = N_HEADS - H_SB
D_SB = H_SB * HEAD_DIM
D_FOX = H_FOX * HEAD_DIM
D_IN = 3 * D_SB + 3 * D_FOX + H_FOX
SCALE = HEAD_DIM ** -0.5
Q_BLOCK = 128
N_GROUPS = 4
EXPERTS_PER_GROUP = 8
N_EXPERTS = N_GROUPS * EXPERTS_PER_GROUP
D_EXPERT = D_MODEL // 8
TOP_K_EXPERT = 2
RMS_EPS = 1e-6

kernel_name = "hymba_style_stickbreak_fox_hmoe_step"

def rms_norm(x, g):
    xf = x.astype(jnp.float32)
    y = xf * lax.rsqrt(jnp.mean(xf * xf, axis=-1, keepdims=True) + RMS_EPS)
    return (y * g.astype(jnp.float32)).astype(x.dtype)

def project(u, w_in, b_forget):
    B, S, _ = u.shape
    z = jnp.einsum('bsd,de->bse', u, w_in)
    cuts = [int(c) for c in np.cumsum([D_SB, D_SB, D_SB, D_FOX, D_FOX, D_FOX])]
    q_sb, k_sb, v_sb, q_fx, k_fx, v_fx, f = jnp.split(z, cuts, axis=-1)
    sb = lambda t: t.reshape(B, S, H_SB, HEAD_DIM)
    fx = lambda t: t.reshape(B, S, H_FOX, HEAD_DIM)
    logf = jax.nn.log_sigmoid((f + b_forget).astype(jnp.float32))
    return sb(q_sb), sb(k_sb), sb(v_sb), fx(q_fx), fx(k_fx), fx(v_fx), logf

def stick_breaking(q, k, v, q_pos, k_pos):
    z = jnp.einsum('bqhd,bkhd->bhqk', q, k, preferred_element_type=jnp.float32) * SCALE
    causal = k_pos[None, :] < q_pos[:, None]
    log_stay = jnp.where(causal, jax.nn.log_sigmoid(-z), 0.0)
    later = lax.cumsum(log_stay, axis=3, reverse=True) - log_stay
    a = jnp.where(causal, jnp.exp(jax.nn.log_sigmoid(z) + later), 0.0)
    return jnp.einsum('bhqk,bkhd->bqhd', a.astype(v.dtype), v)

def forgetting(q, k, v, cq, ck, q_pos, k_pos):
    z = jnp.einsum('bqhd,bkhd->bhqk', q, k, preferred_element_type=jnp.float32) * SCALE
    z = z + cq[..., :, None] - ck[..., None, :]
    causal = k_pos[None, :] <= q_pos[:, None]
    p = jax.nn.softmax(jnp.where(causal, z, -jnp.inf), axis=-1)
    return jnp.einsum('bhqk,bkhd->bqhd', p.astype(v.dtype), v)

def merge_heads(o_sb, o_fx, g_sb, g_fx, w_out):
    B, S = o_sb.shape[:2]
    o = jnp.concatenate([rms_norm(o_sb.reshape(B, S, D_SB), g_sb),
                         rms_norm(o_fx.reshape(B, S, D_FOX), g_fx)], axis=-1)
    return jnp.einsum('bse,ed->bsd', o, w_out)

def prompt_attention(u, w_in, b_forget, g_sb, g_fx, w_out):
    B, S, _ = u.shape
    q_sb, k_sb, v_sb, q_fx, k_fx, v_fx, logf = project(u, w_in, b_forget)
    c = jnp.cumsum(logf, axis=1).transpose(0, 2, 1)
    pos = jnp.arange(S)
    nb = S // Q_BLOCK
    blocks = lambda t: t.reshape(B, nb, Q_BLOCK, *t.shape[2:]).swapaxes(0, 1)
    cq_b = c.reshape(B, H_FOX, nb, Q_BLOCK).transpose(2, 0, 1, 3)
    pos_b = pos.reshape(nb, Q_BLOCK)

    def body(xs):
        qs, qf, cq, qp = xs
        return (stick_breaking(qs, k_sb, v_sb, qp, pos),
                forgetting(qf, k_fx, v_fx, cq, c, qp, pos))

    o_sb, o_fx = lax.map(body, (blocks(q_sb), blocks(q_fx), cq_b, pos_b))
    unblock = lambda t: t.swapaxes(0, 1).reshape(B, S, *t.shape[3:])
    y = merge_heads(unblock(o_sb), unblock(o_fx), g_sb, g_fx, w_out)
    return y, (k_sb, v_sb, k_fx, v_fx, logf)

def sample_attention(u, c_sb_k, c_sb_v, c_fx_k, c_fx_v, c_logf, page_table,
                     w_in, b_forget, g_sb, g_fx, w_out):
    B, T, _ = u.shape
    past = page_table.shape[1] * c_sb_k.shape[1]
    q_sb, k_sb, v_sb, q_fx, k_fx, v_fx, logf = project(u, w_in, b_forget)
    gather = lambda cache: cache[page_table].reshape(B, past, *cache.shape[2:])
    k_sb_all = jnp.concatenate([gather(c_sb_k), k_sb], axis=1)
    v_sb_all = jnp.concatenate([gather(c_sb_v), v_sb], axis=1)
    k_fx_all = jnp.concatenate([gather(c_fx_k), k_fx], axis=1)
    v_fx_all = jnp.concatenate([gather(c_fx_v), v_fx], axis=1)
    logf_all = jnp.concatenate([gather(c_logf).astype(jnp.float32), logf], axis=1)
    c = jnp.cumsum(logf_all, axis=1).transpose(0, 2, 1)
    k_pos = jnp.arange(past + T)
    q_pos = past + jnp.arange(T)
    o_sb = stick_breaking(q_sb, k_sb_all, v_sb_all, q_pos, k_pos)
    o_fx = forgetting(q_fx, k_fx_all, v_fx_all, c[:, :, past:], c, q_pos, k_pos)
    y = merge_heads(o_sb, o_fx, g_sb, g_fx, w_out)
    return y, (k_sb, v_sb, k_fx, v_fx, logf)

def hier_moe(u, w_rg, b_rg, w_re, b_re, w_gate, w_up, w_down):
    uf = u.astype(jnp.float32)
    lg = uf @ w_rg.astype(jnp.float32) + b_rg.astype(jnp.float32)
    p_group = jax.nn.softmax(lg, axis=-1)
    _, gsel = lax.top_k(lg, 1)
    g1 = jnp.take_along_axis(p_group, gsel, axis=-1)
    le = jnp.einsum('td,gde->tge', uf, w_re.astype(jnp.float32)) + b_re.astype(jnp.float32)
    le_sel = jnp.take_along_axis(le, gsel[:, :, None], axis=1)[:, 0]
    v2, i2 = lax.top_k(le_sel, TOP_K_EXPERT)
    gate = g1 * jax.nn.softmax(v2, axis=-1)
    eid = gsel * EXPERTS_PER_GROUP + i2
    comb = jnp.sum(jax.nn.one_hot(eid, N_EXPERTS, dtype=jnp.float32) * gate[..., None], axis=1)
    h = jax.nn.silu(jnp.einsum('td,edf->tef', u, w_gate)) * jnp.einsum('td,edf->tef', u, w_up)
    h = h * comb[:, :, None].astype(h.dtype)
    return jnp.einsum('tef,efd->td', h, w_down)

def setup_inputs(seed: int = 0) -> dict:
    key = jax.random.key(seed)
    ks = jax.random.split(key, 24)
    n_pages = PAST_LEN // PAGE_SIZE
    n_used = DEC_BATCH * n_pages
    n_phys = n_used + max(1, n_used // 4)
    nrm = lambda k, shape, s=1.0: jax.random.normal(k, shape, jnp.float32) * s
    ds = D_MODEL ** -0.5
    page_table = jax.random.permutation(ks[0], n_phys)[:n_used].astype(jnp.int32).reshape(DEC_BATCH, n_pages)
    return {
        "x_prompt": nrm(ks[1], (BATCH, SEQ, D_MODEL)),
        "x_sample": nrm(ks[2], (DEC_BATCH, DEC_SEQ, D_MODEL)),
        "cache_sb_k": nrm(ks[3], (DEPTH, n_phys, PAGE_SIZE, H_SB, HEAD_DIM)),
        "cache_sb_v": nrm(ks[4], (DEPTH, n_phys, PAGE_SIZE, H_SB, HEAD_DIM)),
        "cache_fox_k": nrm(ks[5], (DEPTH, n_phys, PAGE_SIZE, H_FOX, HEAD_DIM)),
        "cache_fox_v": nrm(ks[6], (DEPTH, n_phys, PAGE_SIZE, H_FOX, HEAD_DIM)),
        "cache_fox_logf": jax.nn.log_sigmoid(3.0 + nrm(ks[7], (DEPTH, n_phys, PAGE_SIZE, H_FOX), 0.5)),
        "page_table": page_table,
        "norm_attn_g": 1.0 + nrm(ks[8], (DEPTH, D_MODEL), 0.02),
        "w_in": nrm(ks[9], (DEPTH, D_MODEL, D_IN), ds),
        "b_forget": 3.0 + nrm(ks[10], (DEPTH, H_FOX), 0.5),
        "g_sb_out": 1.0 + nrm(ks[11], (DEPTH, D_SB), 0.02),
        "g_fox_out": 1.0 + nrm(ks[12], (DEPTH, D_FOX), 0.02),
        "w_out": nrm(ks[13], (DEPTH, D_MODEL, D_MODEL), ds),
        "norm_ffn_g": 1.0 + nrm(ks[14], (DEPTH, D_MODEL), 0.02),
        "w_router_group": nrm(ks[15], (DEPTH, D_MODEL, N_GROUPS), ds),
        "b_router_group": nrm(ks[16], (DEPTH, N_GROUPS), 0.01),
        "w_router_expert": nrm(ks[17], (DEPTH, N_GROUPS, D_MODEL, EXPERTS_PER_GROUP), ds),
        "b_router_expert": nrm(ks[18], (DEPTH, N_GROUPS, EXPERTS_PER_GROUP), 0.01),
        "w_expert_gate": nrm(ks[19], (DEPTH, N_EXPERTS, D_MODEL, D_EXPERT), ds),
        "w_expert_up": nrm(ks[20], (DEPTH, N_EXPERTS, D_MODEL, D_EXPERT), ds),
        "w_expert_down": nrm(ks[21], (DEPTH, N_EXPERTS, D_EXPERT, D_MODEL), D_EXPERT ** -0.5),
        "norm_final_g": 1.0 + nrm(ks[22], (D_MODEL,), 0.02),
    }

def reference(x_prompt, x_sample, cache_sb_k, cache_sb_v, cache_fox_k, cache_fox_v,
              cache_fox_logf, page_table, norm_attn_g, w_in, b_forget, g_sb_out,
              g_fox_out, w_out, norm_ffn_g, w_router_group, b_router_group,
              w_router_expert, b_router_expert, w_expert_gate, w_expert_up,
              w_expert_down, norm_final_g):
    B, S, D = x_prompt.shape
    DB, DS, _ = x_sample.shape
    hp, hs = x_prompt, x_sample
    new_p, new_s = [], []
    for l in range(DEPTH):
        yp, st_p = prompt_attention(rms_norm(hp, norm_attn_g[l]), w_in[l], b_forget[l],
                                    g_sb_out[l], g_fox_out[l], w_out[l])
        ys, st_s = sample_attention(rms_norm(hs, norm_attn_g[l]), cache_sb_k[l], cache_sb_v[l],
                                    cache_fox_k[l], cache_fox_v[l], cache_fox_logf[l], page_table,
                                    w_in[l], b_forget[l], g_sb_out[l], g_fox_out[l], w_out[l])
        hp = hp + yp
        hs = hs + ys
        u = jnp.concatenate([rms_norm(hp, norm_ffn_g[l]).reshape(B * S, D),
                             rms_norm(hs, norm_ffn_g[l]).reshape(DB * DS, D)], axis=0)
        f = hier_moe(u, w_router_group[l], b_router_group[l], w_router_expert[l],
                     b_router_expert[l], w_expert_gate[l], w_expert_up[l], w_expert_down[l])
        hp = hp + f[:B * S].reshape(B, S, D)
        hs = hs + f[B * S:].reshape(DB, DS, D)
        new_p.append(st_p)
        new_s.append(st_s)
    y_prompt = rms_norm(hp, norm_final_g)
    y_sample = rms_norm(hs, norm_final_g)
    sb_k_prompt = jnp.stack([s[0] for s in new_p])
    sb_v_prompt = jnp.stack([s[1] for s in new_p])
    fox_k_prompt = jnp.stack([s[2] for s in new_p])
    fox_v_prompt = jnp.stack([s[3] for s in new_p])
    fox_logf_prompt = jnp.stack([s[4] for s in new_p])
    sb_k_sample = jnp.stack([s[0] for s in new_s])
    sb_v_sample = jnp.stack([s[1] for s in new_s])
    fox_k_sample = jnp.stack([s[2] for s in new_s])
    fox_v_sample = jnp.stack([s[3] for s in new_s])
    fox_logf_sample = jnp.stack([s[4] for s in new_s])
    return (y_prompt, y_sample, sb_k_prompt, sb_v_prompt, fox_k_prompt, fox_v_prompt,
            fox_logf_prompt, sb_k_sample, sb_v_sample, fox_k_sample, fox_v_sample,
            fox_logf_sample)


_drawn_inputs = setup_inputs


def setup_inputs(seed=0):
    import zlib

    import numpy as np

    out = dict(_drawn_inputs(seed))
    spreads = {}
    factors = {'g_sb_out': 4.413,
     'b_router_group': 48.017,
     'norm_final_g': 7.909,
     'g_fox_out': 7.379,
     'norm_ffn_g': 3.379,
     'b_router_expert': 8.0}
    for name, (base, spread) in spreads.items():
        noise = np.random.default_rng([zlib.crc32(name.encode()), seed]).standard_normal(out[name].shape)
        drawn = base * np.exp(spread * noise) if base else spread * noise
        out[name] = __import__('jax').numpy.asarray(drawn.astype(out[name].dtype))
    for name, factor in factors.items():
        out[name] = (out[name] * factor).astype(out[name].dtype)
    return out
```

```python
from contextlib import ExitStack

import concourse.bass as bass
from concourse import mybir

F32 = mybir.dt.float32
I32 = mybir.dt.int32
ALU = mybir.AluOpType
ACT = mybir.ActivationFunctionType
AX = mybir.AxisListType.X

P = 128
D = 2048
SEQ = 256
NB = 8
T = SEQ + NB
HD = 128
H = 8
KC = D // P
PAGES = 16
SCALE = HD ** -0.5
EPS = 1e-6
NG = 4
EPG = 8
NE = NG * EPG
FE = D // 8
SLOTS = 64
EXTRA = 8
BLOCKS = NE + EXTRA
PAIRS = BLOCKS // 2
NEG = -1.0e30
TILES = [(0, P), (P, P), (SEQ, NB)]


class Steps:

    def __init__(self, eng, sem):
        self.eng, self.sem, self.base, self.n = eng, sem, 0, 0

    def step(self, ins):
        self.n += 1
        ins.then_inc(self.sem, 1)
        self.eng.wait_ge(self.sem, self.base + self.n)

    def enter(self, i, per_turn):
        self.start = self.base + self.n
        self.base, self.n, self.per_turn = self.start + i * per_turn, 0, per_turn

    def leave(self, turns):
        assert self.n == self.per_turn, f"steps in a turn: {self.n}, not {self.per_turn}"
        self.base, self.n = self.start + turns * self.per_turn, 0


def done_with(nc, sems):
    nc.clear_and_free_semaphores(list(sems.values()))
    nc.all_engine_barrier()


def at(buf, i, lo, hi):
    return buf[:, bass.ds(i, 1), lo:hi].rearrange("p a f -> p (a f)")


def over(ap, n):
    s = list(ap.shape)
    return ap.rearrange("p (a o) -> p a o", o=1).to_broadcast([s[0], s[1], n])


def hybrid_step(nc, a, outs, u_rows, h_rows, y_rows):
    (y_prompt, y_sample, sbk_p, sbv_p, fxk_p, fxv_p, logf_p, sbk_s, sbv_s, fxk_s, fxv_s, logf_s) = outs
    ctx = ExitStack()
    with ctx:
        def sem(name):
            return nc.alloc_semaphore(name=name)

        def sb(name, shape, dt=F32, where=ctx):
            return where.enter_context(nc.sbuf_tensor(name, shape, dt))

        bank = [ctx.enter_context(nc.psum_tensor(f"bank{i}", [P, 512], F32)) for i in range(8)]

        ident = sb("ident", [P, P])
        ones = sb("ones", [P, P])
        tri_ge = sb("tri_ge", [P, P])
        tri_gt = sb("tri_gt", [P, P])
        tri_le = sb("tri_le", [P, P])
        tri_lt = sb("tri_lt", [P, P])
        neg_sb = sb("neg_sb", [P, P])
        neg_fx = sb("neg_fx", [P, P])
        later = sb("later", [P, P])
        pick4 = sb("pick4", [P, 4, H])
        pick = sb("pick", [P, H])
        seg = sb("seg", [P, H, PAGES + 1])
        gcol = sb("gcol", [P, 48])
        G_ATTN, G_FFN, G_GRP = 0, 16, 32
        xT = sb("xT", [P, KC, T])
        xn = sb("xn", [P, KC, T])
        qo = sb("qo", [P, 2 * H, T])
        lf = sb("lf", [P, 3, H])
        wr = sb("wr", [P, KC, NG + NE])
        br = sb("br", [P, NG + NE])

        s_const = sem("s_const")

        bctx = ExitStack()
        ctx.enter_context(bctx)
        qrow = sb("qrow", [NB, 2 * H * HD], where=bctx)
        cTs = sb("cTs", [H, SEQ], where=bctx)
        FB = sb("FB", [P, NB, H * PAGES], where=bctx)
        ptr = sb("ptr", [1, NB * PAGES], I32, where=bctx)

        actx = ExitStack()
        xrow = sb("xrow", [P, 3, D], where=actx)
        sq = sb("sq", [P, KC * T], where=actx)
        wq = sb("wq", [P, 4, KC, 256], where=actx)
        grow = sb("grow", [48, P], where=actx)
        ptc = sb("ptc", [P, 1], I32, where=actx)
        wf = sb("wf", [P, KC, H], where=actx)
        bf = sb("bf", [P, H], where=actx)
        rst = sb("rst", [P, T], where=actx)
        rstd = sb("rstd", [P, T], where=actx)
        fl = sb("fl", [P, 3 * H], where=actx)
        fa = sb("fa", [P, 3 * H], where=actx)
        fr = sb("fr", [P, 3 * H], where=actx)
        lfr = sb("lfr", [P, P * H], where=actx)
        LFT = sb("LFT", [P, H * P], where=actx)
        ltot = sb("ltot", [P, H], where=actx)
        totb = sb("totb", [P, H, P], where=actx)

        A = {n: sem("a_" + n) for n in (
            "x0 x1 x2 g_in pt_in ptc_in wf_in bf_in wr_in tpose tcopy gt sq ss ms sqrt rstd xn f fl fln "
            "lf q_done q_evac qr qrc lft ltc tot ct ctc fb fbc lfg lst w0 w1 w2 w3 pool dve act").split()}
        w_in = a["w_in"][0].rearrange("(c p) n -> p c n", p=P)

        with nc.Block() as block:
            @block.sync
            def _(sp):
                for t, (lo, n) in enumerate(TILES):
                    src = a["x_prompt"][0, lo:lo + n] if t < 2 else a["x_sample"].rearrange("b s d -> (b s) d")
                    sp.dma_start(xrow[0:n, t, :], src).then_inc(A[f"x{t}"], 16)
                for i, (name, r0, r1) in enumerate((("norm_attn_g", 0, 16), ("norm_ffn_g", 16, 32),
                                                    ("g_sb_out", 32, 40), ("g_fox_out", 40, 48))):
                    sp.dma_start(grow[r0:r1, :], a[name][0].rearrange("(c p) -> c p", p=P)).then_inc(A["g_in"], 16)
                for n in range(8):
                    if n >= 4:
                        sp.wait_ge(A["q_done"], 2 * (n - 4) + 2)
                    c0 = (n // 4) * 3 * H * HD + (n % 4) * 256
                    sp.dma_start(wq[:, n % 4, :, :], w_in[:, :, c0:c0 + 256]).then_inc(A[f"w{n % 4}"], 16)
                sp.wait_ge(A["lf"], 1)
                sp.dma_start(logf_p[0, 0].rearrange("(t p) h -> p t h", p=P), lf[:, 0:2, :]).then_inc(A["lst"], 16)
                sp.dma_start(logf_s[0].rearrange("b s h -> (b s) h"), lf[0:NB, 2, :]).then_inc(A["lst"], 16)
                sp.wait_ge(A["lst"], 32)

            @block.gpsimd
            def _(pool):
                own = Steps(pool, A["pool"])
                own.step(pool.memset(ones[:, :], 1.0))
                own.step(pool.memset(neg_sb[:, :], 0.0))

                def select(out, src, op, base, pattern, mult, fill):
                    own.step(pool.affine_select(out=out, in_=src, compare_op=op, fill=fill, base=base,
                                                pattern=pattern, channel_multiplier=mult))
                select(ident[:, :], ones[:, :], ALU.is_equal, 0, [[-1, P]], 1, 0.0)
                select(tri_ge[:, :], ones[:, :], ALU.is_ge, 0, [[-1, P]], 1, 0.0)
                select(tri_gt[:, :], ones[:, :], ALU.is_ge, -1, [[-1, P]], 1, 0.0)
                select(tri_le[:, :], ones[:, :], ALU.is_ge, 0, [[1, P]], -1, 0.0)
                select(tri_lt[:, :], ones[:, :], ALU.is_ge, -1, [[1, P]], -1, 0.0)
                select(neg_fx[:, :], neg_sb[:, :], ALU.is_ge, 0, [[-1, P]], 1, NEG)
                select(neg_sb[:, :], neg_sb[:, :], ALU.is_ge, -1, [[1, P]], -1, NEG)
                lv = later[:, :].rearrange("p (b j) -> p b j", j=PAGES)
                ov = ones[:, :].rearrange("p (b j) -> p b j", j=PAGES)
                select(lv, ov, ALU.is_ge, -1, [[PAGES, NB], [1, PAGES]], -1, 0.0)
                select(lv, lv, ALU.is_ge, 0, [[-PAGES, NB], [0, PAGES]], 1, 0.0)
                select(pick4[:, :, :], ones[:, 0:32].rearrange("p (a h) -> p a h", h=H), ALU.is_equal, 0,
                       [[-32, 4], [-1, H]], 1, 0.0)
                own.step(pool.memset(seg[:, :, :], 1.0))
                own.step(pool.memset(seg[:, :, 0:1], 0.0))
                own.step(pool.memset(fl[:, :], 0.0))
                own.step(pool.memset(lf[:, :, :], 0.0))
                pool.memset(ltot[:, :], 0.0).then_inc(s_const, 1)
                pool.wait_ge(A["ptc_in"], 16)
                pool.indirect_dma_start(
                    lfr[:, :], None, a["cache_fox_logf"][0].rearrange("n p h -> n (p h)"),
                    bass.IndirectOffsetOnAxis(ap=ptc[:, 0:1], axis=0)).then_inc(A["lfg"], 16)

            @block.scalar
            def _(act):
                own = Steps(act, A["act"])
                act.dma_start(ptc[:, :], a["pages"].rearrange("a (n o) -> (a n) o", o=1)).then_inc(A["ptc_in"], 16)
                act.dma_start(ptr[:, :], a["pages"]).then_inc(A["pt_in"], 16)
                act.dma_start(wf[:, :, :], w_in[:, :, 6 * H * HD:6 * H * HD + H]).then_inc(A["wf_in"], 16)
                act.dma_start(bf[:, :], a["b_forget"].to_broadcast([P, H])).then_inc(A["bf_in"], 16)
                act.dma_start(wr[:, :, 0:NG], a["w_router_group"][0].rearrange("(c p) g -> p c g", p=P)).then_inc(A["wr_in"], 16)
                for g in range(NG):
                    act.dma_start(wr[:, :, NG + g * EPG:NG + (g + 1) * EPG],
                                  a["w_router_expert"][0, g].rearrange("(c p) e -> p c e", p=P)).then_inc(A["wr_in"], 16)
                act.dma_start(br[:, 0:NG], a["b_router_group"].to_broadcast([P, NG])).then_inc(A["wr_in"], 16)
                act.dma_start(br[:, NG:NG + NE],
                              a["b_router_expert"].rearrange("l g e -> l (g e)").to_broadcast([P, NE])).then_inc(A["wr_in"], 16)
                act.wait_ge(A["tcopy"], KC)
                nc.scalar.activation(sq[:, :], xT[:, :, :].rearrange("p c t -> p (c t)"), ACT.Square).then_inc(A["sq"], 1)
                act.wait_ge(A["ms"], 1)
                nc.scalar.activation(rst[:, :], rst[:, :], ACT.Sqrt).then_inc(A["sqrt"], 1)
                act.wait_ge(A["fl"], 2)
                own.step(nc.scalar.activation(fa[:, :], fl[:, :], ACT.Abs))
                own.step(nc.scalar.activation(fa[:, :], fa[:, :], ACT.Exp, scale=-1.0))
                nc.scalar.activation(fa[:, :], fa[:, :], ACT.Ln, bias=1.0).then_inc(A["fln"], 1)
                with act.Fori(0, 2) as r:
                    for i in range(H):
                        act.wait_ge(A["q_done"], H * r + i + 1)
                        nc.scalar.activation(at(qo, H * r + i, 0, T), bank[i][:, 0:T], ACT.Copy).then_inc(A["q_evac"], 1)
                act.wait_ge(A["wr_in"], 16 * 7)
                act.wait_ge(A["pt_in"], 16)

            @block.tensor
            def _(pe):
                pe.wait_ge(s_const, 1)
                for t in range(3):
                    pe.wait_ge(A[f"x{t}"], 16)
                for c in range(KC):
                    if c >= 4:
                        pe.wait_ge(A["tcopy"], c - 3)
                    for t, (lo, n) in enumerate(TILES):
                        mm = pe.transpose(bank[c % 4][:, lo:lo + n], xrow[0:n, t, c * P:(c + 1) * P], ident[0:n, 0:n])
                    mm.then_inc(A["tpose"], 1)
                pe.wait_ge(A["g_in"], 64)
                pe.transpose(bank[4][:, 0:48], grow[:, :], ident[0:48, 0:48]).then_inc(A["gt"], 1)
                pe.wait_ge(A["sq"], 1)
                for c in range(KC):
                    mm = pe.matmul(bank[5][:, 0:T], ones[:, :], sq[:, c * T:(c + 1) * T], start=(c == 0), stop=(c == KC - 1))
                mm.then_inc(A["ss"], 1)
                pe.wait_ge(A["xn"], KC)
                pe.wait_ge(A["wf_in"], 16)
                for t, (lo, n) in enumerate(TILES):
                    for c in range(KC):
                        mm = pe.matmul(bank[6][0:n, t * H:(t + 1) * H], xn[:, c, lo:lo + n], wf[:, c, :],
                                       start=(c == 0), stop=(c == KC - 1))
                mm.then_inc(A["f"], 1)
                pe.wait_ge(A["fl"], 2)
                with pe.Fori(0, 2) as r:
                    pe.wait_ge(A["q_evac"], H * r)
                    for j in range(4):
                        pe.wait_ge(A[f"w{j}"], 16 * r + 16)
                        for m in range(2):
                            for c in range(KC):
                                mm = pe.matmul(bank[2 * j + m][:, 0:T], wq[:, j, c, m * P:(m + 1) * P], xn[:, c, :],
                                               start=(c == 0), stop=(c == KC - 1))
                            mm.then_inc(A["q_done"], 1)
                pe.wait_ge(A["q_evac"], 2 * H)
                for h in range(2 * H):
                    mm = pe.transpose(bank[h // 4][0:NB, (h % 4) * P:(h % 4 + 1) * P], qo[:, h, SEQ:T], ident[:, :])
                mm.then_inc(A["qr"], 1)
                pe.wait_ge(A["lfg"], 16)
                lv = lfr[:, :].rearrange("n (p h) -> n h p", h=H)
                for h in range(H):
                    mm = pe.transpose(bank[4 + h // 4][:, (h % 4) * P:(h % 4 + 1) * P], lv[:, h, :], ident[:, :])
                mm.then_inc(A["lft"], 1)
                pe.wait_ge(A["lf"], 1)
                pe.matmul(bank[6][0:H, 0:P], lf[:, 0, :], tri_le[:, :], start=True, stop=True)
                pe.matmul(bank[6][0:H, P:SEQ], lf[:, 0, :], ones[:, :], start=True, stop=False)
                pe.matmul(bank[6][0:H, P:SEQ], lf[:, 1, :], tri_le[:, :], start=False, stop=True).then_inc(A["ct"], 1)
                pe.wait_ge(A["ltc"], 2)
                pe.wait_ge(A["tot"], 1)
                for half in range(2):
                    out = bank[4 + half]
                    pe.matmul(out[:, :], tri_gt[:, :], LFT[:, half * 512:(half + 1) * 512], start=True, stop=False,
                              skip_group_check=True)
                    for k in range(4):
                        mm = pe.matmul(out[:, k * P:(k + 1) * P], totb[:, half * 4 + k, :], later[:, :],
                                       start=False, stop=(k == 3), skip_group_check=True)
                mm.then_inc(A["fb"], 1)

            @block.vector
            def _(dve):
                own = Steps(dve, A["dve"])
                for c in range(KC):
                    dve.wait_ge(A["tpose"], c + 1)
                    dve.tensor_copy(xT[:, c, :], bank[c % 4][:, 0:T]).then_inc(A["tcopy"], 1)
                dve.wait_ge(s_const, 1)
                own.step(dve.tensor_reduce(pick[:, :], pick4[:, :, :].rearrange("p a h -> p h a"), AX, ALU.add))
                dve.wait_ge(A["gt"], 1)
                own.step(dve.tensor_copy(gcol[:, :], bank[4][:, 0:48]))
                dve.wait_ge(A["ss"], 1)
                dve.tensor_scalar(rst[:, :], bank[5][:, 0:T], 1.0 / D, EPS, ALU.mult, ALU.add).then_inc(A["ms"], 1)
                dve.wait_ge(A["sqrt"], 1)
                own.step(dve.reciprocal(rstd[:, :], rst[:, :]))
                for c in range(KC):
                    dve.scalar_tensor_tensor(out=xn[:, c, :], in0=xT[:, c, :], scalar=gcol[:, G_ATTN + c:G_ATTN + c + 1],
                                             in1=rstd[:, :], op0=ALU.mult, op1=ALU.mult).then_inc(A["xn"], 1)
                dve.wait_ge(A["f"], 1)
                dve.wait_ge(A["bf_in"], 16)
                bfv = bf[:, :].rearrange("p (t h) -> p t h", t=1)
                dve.tensor_tensor(fl[:, 0:2 * H].rearrange("p (t h) -> p t h", h=H),
                                  bank[6][:, 0:2 * H].rearrange("p (t h) -> p t h", h=H),
                                  bfv.to_broadcast([P, 2, H]), ALU.add).then_inc(A["fl"], 1)
                dve.tensor_tensor(fl[0:NB, 2 * H:3 * H], bank[6][0:NB, 2 * H:3 * H], bf[0:NB, :], ALU.add).then_inc(A["fl"], 1)
                dve.wait_ge(A["fl"], 2)
                own.step(dve.tensor_scalar(fr[:, :], fl[:, :], -1.0, 0.0, ALU.mult, ALU.max))
                dve.wait_ge(A["fln"], 1)
                dve.scalar_tensor_tensor(out=lf[:, :, :].rearrange("p t h -> p (t h)"), in0=fr[:, :], scalar=-1.0,
                                         in1=fa[:, :], op0=ALU.mult, op1=ALU.subtract).then_inc(A["lf"], 1)
                dve.wait_ge(A["qr"], 1)
                for i in range(4):
                    dve.tensor_copy(qrow[:, i * 512:(i + 1) * 512], bank[i][0:NB, :]).then_inc(A["qrc"], 1)
                dve.wait_ge(A["lft"], 1)
                for i in range(2):
                    dve.tensor_copy(LFT[:, i * 512:(i + 1) * 512], bank[4 + i][:, :]).then_inc(A["ltc"], 1)
                own.step(dve.tensor_reduce(ltot[:, :], lfr[:, :].rearrange("n (p h) -> n h p", h=H), AX, ALU.add))
                dve.tensor_copy(totb[:, :, :], over(ltot[:, :], P)).then_inc(A["tot"], 1)
                dve.wait_ge(A["ct"], 1)
                dve.tensor_scalar(cTs[:, :], bank[6][0:H, 0:SEQ], -1.0 / SCALE, None, ALU.mult).then_inc(A["ctc"], 1)
                dve.wait_ge(A["fb"], 1)
                for i in range(2):
                    dve.tensor_copy(
                        FB[:, :, i * 64:(i + 1) * 64].rearrange("p b (h j) -> p h b j", j=PAGES),
                        bank[4 + i][:, :].rearrange("p (h b j) -> p h b j", h=4, j=PAGES)).then_inc(A["fbc"], 1)
                dve.wait_ge(A["fbc"], 2)
        actx.close()
        done_with(nc, A)

        attention(nc, a, ident, ones, tri_ge, tri_lt, neg_sb, neg_fx, pick, seg, xn, qo, lf, qrow, cTs, FB, ptr,
                  w_in, bank, sem, outs)
        bctx.close()
        ffn(nc, ctx, a, ident, ones, tri_lt, gcol, xT, xn, qo, wr, br, bank, sem, y_prompt, y_sample,
            u_rows, h_rows, y_rows)


DVE_TURN = 22
ACT_TURN = 4


def attention(nc, a, ident, ones, tri_ge, tri_lt, neg_sb, neg_fx, pick, seg, xn, qo, lf, qrow, cTs, FB, ptr,
              w_in, bank, sem, outs):
    (_, _, sbk_p, sbv_p, fxk_p, fxv_p, _, sbk_s, sbv_s, fxk_s, fxv_s, _) = outs
    ctx = ExitStack()
    with ctx:
        def sb(name, shape, dt=F32):
            return ctx.enter_context(nc.sbuf_tensor(name, shape, dt))

        kring = sb("kring", [P, 4, 2, H * HD])
        vring = sb("vring", [P, 4, 2, H * HD])
        wkv = sb("wkv", [P, 2, KC, HD])
        qb = sb("qb", [P, 2 * H * HD])
        osum = sb("osum", [P, 4, 512])
        kT = [sb(f"kT{g}", [P, T]) for g in range(2)]
        vT = [sb(f"vT{g}", [P, T]) for g in range(2)]
        krow = [sb(f"krow{g}", [P, 3, HD]) for g in range(2)]
        vrow = [sb(f"vrow{g}", [P, 3, HD]) for g in range(2)]
        qf = sb("qf", [P, SEQ])
        cm = sb("cm", [H, SEQ])
        ecol = sb("ecol", [H, 1])
        stay = sb("stay", [P, 384])
        pos_z = sb("pos_z", [P, 384])
        att = sb("att", [P, 384])
        zf = sb("zf", [P, 384])
        pf = sb("pf", [P, 384])
        pT = sb("pT", [P, 384])
        nmax = sb("nmax", [P, 2])
        rsum = sb("rsum", [P, 2])
        rinv = sb("rinv", [P, 2])
        sel = sb("sel", [NB, P])
        Z = sb("Z", [P, 2, H, PAGES])
        zs = sb("zs", [P, H * PAGES])
        zr = sb("zr", [P, H * PAGES])
        sp_h = sb("sp_h", [P, H, PAGES + 1])
        run = sb("run", [P, H, PAGES + 1])
        ts = sb("ts", [P, H * PAGES])
        zx = sb("zx", [P, H * PAGES])
        mxp = sb("mxp", [P, H])
        m8 = sb("m8", [H, 1])
        diag = sb("diag", [H, H])
        dsum = sb("dsum", [P, H])
        PR = sb("PR", [P, 2, PAGES, 32])
        MX = sb("MX", [P, NB, H])
        DEN = sb("DEN", [P, NB, H])
        OF = sb("OF", [P, NB, H])
        QK = sb("QK", [P, H, NB])
        VN = sb("VN", [P, H, NB])
        fin = [sb(f"fin{i}", [P, H * NB]) for i in range(6)]
        ab = sb("ab", [P, 2, H * NB])
        dlf = sb("dlf", [NB, H, NB])

        S = {n: sem("b_" + n) for n in (
            "k0 k1 k2 k3 v0 v1 v2 v3 kused vused w0 w1 pad "
            "sel bcast qb proj0 proj1 proj2 proj3 kv0 kv1 kv2 kv3 tr0 tr1 tr2 tr3 row0 row1 row2 row3 "
            "st0 st1 st2 st3 qf cm sbz sln sp C t at fxz zf fp pn sbo sboc tp pT fxo fxoc own_kv "
            "mx ssl ssp mxT diag mb zx C2 ts w_fx w_sb dsum osum ext extc den denc done1 done2 done3 "
            "dve act pool lfd").split()}
        caches = [a["cache_sb_k"][0], a["cache_fox_k"][0]], [a["cache_sb_v"][0], a["cache_fox_v"][0]]
        caches = [[c.rearrange("n p h d -> n p (h d)") for c in cs] for cs in caches]
        n_phys = a["cache_sb_k"].shape[1]
        GR = PAGES // 4

        bstack = ExitStack()
        block = bstack.enter_context(nc.Block())

        @block.sync
        def _(sp):
            def load(kv, page, slot):
                ring, s = (kring, S[f"k{slot}"]) if kv == 0 else (vring, S[f"v{slot}"])
                for g in range(2):
                    sp.dma_start(ring[:, slot, g, :],
                                 caches[kv][g][bass.ds(page, 1)].rearrange("a p f -> (a p) f")).then_inc(s, 16)

            def page_of(i):
                return sp.value_load(ptr[0:1, bass.ds(i, 1)], min_val=0, max_val=n_phys - 1)

            def keys(g, first=False):
                for u in range(4):
                    if not first:
                        sp.wait_ge(S["kused"], 4 * (g - 1) + u + 1)
                    load(0, page_of(4 * g + u), u)

            def both(g, first=False):
                for u in range(4):
                    if not first:
                        sp.wait_ge(S["vused"], 4 * (g - GR - 1) + u + 1)
                    load(1, page_of(4 * (g - GR) + u), u)
                    sp.wait_ge(S["kused"], 4 * (g - 1) + u + 1)
                    load(0, page_of(4 * g + u), u)

            keys(0, first=True)
            with sp.Fori(1, GR) as g:
                keys(g)
            both(GR, first=True)
            with sp.Fori(GR + 1, NB * GR) as g:
                both(g)
            with sp.Fori(NB * GR, (NB + 1) * GR) as g:
                for u in range(4):
                    sp.wait_ge(S["vused"], 4 * (g - GR - 1) + u + 1)
                    load(1, page_of(4 * (g - GR) + u), u)

        @block.gpsimd
        def _(pool):
            own = Steps(pool, S["pool"])
            own.step(pool.memset(PR[:, :, :, :], 0.0))
            pool.memset(sp_h[:, :, :], 0.0).then_inc(S["pad"], 1)

            def select_sample(n, first=False):
                if not first:
                    pool.wait_ge(S["bcast"], n)
                pool.tensor_copy(sel[:, :], ident[0:NB, bass.ds(n, 1)].to_broadcast([NB, P])).then_inc(S["sel"], 1)

            select_sample(0, first=True)
            select_sample(1)

            def turn(b, last):
                pool.wait_ge(S["cm"], b)
                pool.wait_ge(S["fxz"], b)
                pool.tensor_copy(qf[:, :], at(qo, b + H, 0, SEQ)).then_inc(S["qf"], 1)
                own.step(pool.tensor_copy(ecol[:, :], ident[0:H, bass.ds(b, 1)]))
                pool.tensor_tensor(cm[:, :], cTs[:, :], ecol[:, 0:1].to_broadcast([H, SEQ]), ALU.mult).then_inc(S["cm"], 1)
                if not last:
                    select_sample(b + 2)

            with pool.Fori(0, NB - 1) as b:
                own.enter(b, 1)
                turn(b, False)
            own.leave(NB - 1)
            turn(NB - 1, True)

        @block.tensor
        def _(pe):
            def project(i, b):
                pe.wait_ge(S[f"w{i % 2}"], 32 * b + 16 * (i // 2) + 16)
                out = bank[4 + i % 2]
                for c in range(KC):
                    mm = pe.matmul(out[:, 0:T], wkv[:, i % 2, c, :], xn[:, c, :], start=(c == 0), stop=(c == KC - 1))
                mm.then_inc(S[f"proj{i}"], 1)

            def rows(i, src, out, b):
                pe.wait_ge(S[f"kv{i}"], b + 1)
                for t, (lo, n) in enumerate(TILES):
                    mm = pe.transpose(out[0:n, t * P:(t + 1) * P], src[:, lo:lo + n], ident[:, :])
                mm.then_inc(S[f"tr{i}"], 1)

            def values(b, q):
                for u in range(4):
                    t = 4 * q + u
                    pe.wait_ge(S[f"v{u}"], 32 * (4 * b + q + 1))
                    for g in range(2):
                        for half in range(2):
                            mm = pe.matmul(bank[2 * g + half][32 * u:32 * u + 32, :], PR[:, g, t, :],
                                           vring[:, u, g, half * 512:(half + 1) * 512],
                                           start=(t < 4), stop=(t >= PAGES - 4))
                    mm.then_inc(S["vused"], 1)

            def broadcast(n):
                pe.wait_ge(S["sel"], n + 1)
                for i in range(4):
                    mm = pe.matmul(bank[4 + i][:, :], sel[:, :], qrow[:, i * 512:(i + 1) * 512], start=True, stop=True)
                mm.then_inc(S["bcast"], 1)

            def weights(n, extract):
                pe.wait_ge(S["mx"], n + 1)
                pe.transpose(bank[4][0:H, 0:P], mxp[:, :], ident[:, :]).then_inc(S["mxT"], 1)
                pe.wait_ge(S["ssp"], n + 1)
                pe.matmul(bank[5][:, 0:P], tri_ge[:, :], sp_h[:, :, 1:PAGES + 1], start=True, stop=False)
                pe.matmul(bank[5][:, 0:P], ones[:, :], run[:, :, 0:PAGES], start=False, stop=True).then_inc(S["C2"], 1)
                pe.wait_ge(S["diag"], n + 1)
                pe.matmul(bank[4][:, P:P + H], ones[0:H, :], diag[:, :], start=True, stop=True).then_inc(S["mb"], 1)
                if extract:
                    outputs(n - 1)
                pe.wait_ge(S["dsum"], n + 1)
                pe.wait_ge(S["ts"], n + 1)
                pe.matmul(bank[5][:, 256:256 + H], ones[:, :], dsum[:, :], start=True, stop=True).then_inc(S["den"], 1)
                pe.wait_ge(S["zx"], n + 1)
                pe.wait_ge(S["denc"], n + 1)

            def outputs(b):
                pe.wait_ge(S["osum"], 4 * b + 4)
                pe.wait_ge(S["sboc"], b + 1)
                for i in range(2 * H):
                    mm = pe.matmul(bank[6][:, i:i + 1], osum[:, i // 4, (i % 4) * P:(i % 4 + 1) * P],
                                   pick[:, i % H:i % H + 1], start=True, stop=True)
                mm.then_inc(S["ext"], 1)

            def prompt_out(row, w, out, done):
                pe.matmul(out[:, 0:SEQ], row[:, 0, :], w[:, 0:SEQ], start=True, stop=False)
                pe.matmul(out[:, P:SEQ], row[:, 1, :], w[:, SEQ:384], start=False, stop=True).then_inc(S[done], 1)

            def turn(b, last):
                pe.wait_ge(S["qb"], 4 * (b + 2))
                project(0, b)
                project(1, b)
                pe.wait_ge(S["w_sb"], b + 1)
                pe.wait_ge(S["w_fx"], b + 1)
                values(b, 0)
                rows(0, kT[0], bank[6], b)
                rows(1, vT[0], bank[7], b)
                pe.wait_ge(S["kv0"], b + 1)
                project(2, b)
                project(3, b)
                pe.wait_ge(S["row0"], b + 1)
                pe.matmul(bank[6][:, 0:SEQ], kT[0][:, 0:P], at(qo, b, 0, SEQ), start=True, stop=True)
                pe.matmul(bank[6][:, SEQ:384], kT[0][:, P:SEQ], at(qo, b, P, SEQ), start=True, stop=True).then_inc(S["sbz"], 1)
                values(b, 1)
                pe.wait_ge(S["row1"], b + 1)
                rows(2, kT[1], bank[7], b)
                rows(3, vT[1], bank[4], b)
                pe.wait_ge(S["kv3"], b + 1)
                pe.wait_ge(S["qf"], b + 1)
                pe.wait_ge(S["cm"], b + 1)
                pe.matmul(bank[5][:, 0:P], qf[:, 0:P], kT[1][:, 0:P], start=True, stop=False)
                pe.matmul(bank[5][:, 0:P], ones[0:H, :], cm[:, 0:P], start=False, stop=True)
                pe.matmul(bank[5][:, P:384], qf[:, P:SEQ], kT[1][:, 0:SEQ], start=True, stop=False)
                pe.matmul(bank[5][:, P:384], ones[0:H, :], cm[:, :], start=False, stop=True).then_inc(S["fxz"], 1)
                pe.wait_ge(S["row2"], b + 1)
                pe.wait_ge(S["sp"], b + 1)
                pe.matmul(bank[7][:, 0:384], tri_ge[:, :], stay[:, :], start=True, stop=False, skip_group_check=True)
                pe.matmul(bank[7][:, P:SEQ], ones[:, :], stay[:, SEQ:384], start=False, stop=True,
                          skip_group_check=True).then_inc(S["C"], 1)
                values(b, 2)
                pe.wait_ge(S["at"], b + 1)
                prompt_out(vrow[0], att, bank[6], "sbo")
                pe.wait_ge(S["row3"], b + 1)
                pe.wait_ge(S["pn"], b + 1)
                for k in range(3):
                    mm = pe.transpose(bank[4][:, k * P:(k + 1) * P], pf[:, k * P:(k + 1) * P], ident[:, :])
                mm.then_inc(S["tp"], 1)
                values(b, 3)
                pe.wait_ge(S["pT"], b + 1)
                prompt_out(vrow[1], pT, bank[7], "fxo")
                if last:
                    outputs(b)
                else:
                    weights(b + 1, True)
                    pe.wait_ge(S["extc"], b + 1)
                    pe.wait_ge(S["fxoc"], b + 1)
                    broadcast(b + 2)

            broadcast(0)
            pe.wait_ge(S["qb"], 4)
            weights(0, False)
            broadcast(1)
            with pe.Fori(0, NB - 1) as b:
                turn(b, False)
            turn(NB - 1, True)
            pe.wait_ge(S["own_kv"], 2 * NB)
            pe.matmul(bank[4][:, 0:64], ones[:, :], QK[:, :, :], start=True, stop=True)
            pe.wait_ge(S["lfd"], 1)
            pe.matmul(bank[4][:, 64:128], ones[0:NB, :], dlf[:, :, :], start=True, stop=True).then_inc(S["done1"], 1)

        @block.scalar
        def _(act):
            own = Steps(act, S["act"])

            def load_w(i, b):
                c0 = (1 + i % 2 + 3 * (i // 2)) * H * HD
                src = w_in[:, :, c0:c0 + H * HD].rearrange("p c (h d) -> h p c d", d=HD)
                act.dma_start(wkv[:, i % 2, :, :], src[bass.ds(b, 1)].rearrange("a p c d -> (a p) c d")).then_inc(S[f"w{i % 2}"], 16)

            def copy(out, src, done):
                nc.scalar.activation(out, src, ACT.Copy).then_inc(S[done], 1)

            def softplus_1(out, z):
                own.step(nc.scalar.activation(out, z, ACT.Abs, scale=SCALE))
                own.step(nc.scalar.activation(out, out, ACT.Exp, scale=-1.0))
                return nc.scalar.activation(out, out, ACT.Ln, bias=1.0)

            def store(i, row, out_p, out_s, b):
                act.wait_ge(S[f"row{i}"], b + 1)
                act.dma_start(out_p[0, 0].rearrange("(t p) h d -> h p t d", p=P)[bass.ds(b, 1)].rearrange("a p t d -> (a p) t d"),
                               row[:, 0:2, :]).then_inc(S[f"st{i}"], 16)
                act.dma_start(out_s[0].rearrange("b s h d -> h (b s) d")[bass.ds(b, 1)].rearrange("a b d -> (a b) d"),
                               row[0:NB, 2, :]).then_inc(S[f"st{i}"], 16)

            def sample_softplus(n):
                act.wait_ge(S["kused"], PAGES * (n + 1))
                softplus_1(zs[:, :], Z[:, 0, :, :].rearrange("p h j -> p (h j)")).then_inc(S["ssl"], 1)

            def sample_weights(n):
                for g, src, ready, done in ((1, zx, "zx", "w_fx"), (0, ts, "ts", "w_sb")):
                    act.wait_ge(S[ready], n + 1)
                    nc.scalar.activation(PR[:, g, :, 0:H].rearrange("p j h -> p h j"),
                                         src[:, :].rearrange("p (h j) -> p h j", j=PAGES), ACT.Exp).then_inc(S[done], 1)

            def queries(n):
                act.wait_ge(S["bcast"], n + 1)
                for i in range(4):
                    copy(qb[:, i * 512:(i + 1) * 512], bank[4 + i][:, :], "qb")

            def turn(b, last):
                act.wait_ge(S["proj0"], b + 1)
                copy(kT[0][:, :], bank[4][:, 0:T], "kv0")
                load_w(2, b)
                act.wait_ge(S["proj1"], b + 1)
                copy(vT[0][:, :], bank[5][:, 0:T], "kv1")
                load_w(3, b)
                act.wait_ge(S["proj2"], b + 1)
                act.wait_ge(S["own_kv"], 2 * b)
                copy(kT[1][:, :], bank[4][:, 0:T], "kv2")
                if not last:
                    load_w(0, b + 1)
                act.wait_ge(S["proj3"], b + 1)
                copy(vT[1][:, :], bank[5][:, 0:T], "kv3")
                if not last:
                    load_w(1, b + 1)
                act.wait_ge(S["sbz"], b + 1)
                softplus_1(stay[:, :], bank[6][:, 0:384]).then_inc(S["sln"], 1)
                act.wait_ge(S["t"], b + 1)
                nc.scalar.activation(att[:, :], att[:, :], ACT.Exp).then_inc(S["at"], 1)
                store(0, krow[0], sbk_p, sbk_s, b)
                store(1, vrow[0], sbv_p, sbv_s, b)
                store(2, krow[1], fxk_p, fxk_s, b)
                store(3, vrow[1], fxv_p, fxv_s, b)
                act.wait_ge(S["zf"], b + 1)
                nc.scalar.activation(pf[:, 0:P], zf[:, 0:P], ACT.Exp, bias=nmax[:, 0:1], accum_out=rsum[:, 0:1]).then_inc(S["fp"], 1)
                nc.scalar.activation(pf[:, P:384], zf[:, P:384], ACT.Exp, bias=nmax[:, 1:2], accum_out=rsum[:, 1:2]).then_inc(S["fp"], 1)
                act.wait_ge(S["sbo"], b + 1)
                copy(at(qo, b, 0, SEQ), bank[6][:, 0:SEQ], "sboc")
                act.wait_ge(S["tp"], b + 1)
                copy(pT[:, :], bank[4][:, 0:384], "pT")
                act.wait_ge(S["fxo"], b + 1)
                act.wait_ge(S["qf"], b + 1)
                copy(at(qo, b + H, 0, SEQ), bank[7][:, 0:SEQ], "fxoc")
                if not last:
                    sample_softplus(b + 1)
                act.wait_ge(S["vused"], PAGES * (b + 1))
                act.wait_ge(S["ext"], b)
                for i in range(4):
                    copy(osum[:, i, :], bank[i][:, :], "osum")
                if not last:
                    sample_weights(b + 1)
                    queries(b + 2)

            load_w(0, 0)
            load_w(1, 0)
            queries(0)
            sample_softplus(0)
            act.wait_ge(S["pad"], 1)
            sample_weights(0)
            act.wait_ge(S["kused"], PAGES)
            queries(1)
            with act.Fori(0, NB - 1) as b:
                own.enter(b, ACT_TURN)
                turn(b, False)
            own.leave(NB - 1)
            turn(NB - 1, True)
            for i in range(4):
                act.wait_ge(S[f"st{i}"], 32 * NB)
            act.wait_ge(S["done2"], 1)
            nc.scalar.activation(ab[:, :, :], ab[:, :, :], ACT.Exp).then_inc(S["done3"], 1)

        @block.vector
        def _(dve):
            own = Steps(dve, S["dve"])

            def score(n, q):
                if q == 0:
                    dve.wait_ge(S["qb"], 4 * (n + 1))
                for u in range(4):
                    dve.wait_ge(S[f"k{u}"], 32 * (4 * n + q + 1))
                    for g in range(2):
                        for h in range(H):
                            k = kring[:, u, g, h * HD:(h + 1) * HD]
                            ins = dve.tensor_tensor_reduce(k, k, qb[:, (g * H + h) * HD:(g * H + h + 1) * HD], 1.0, 0.0,
                                                           ALU.mult, ALU.add, Z[:, g, h, 4 * q + u:4 * q + u + 1])
                    ins.then_inc(S["kused"], 1)

            def by_head(x):
                return x.rearrange("p (h j) -> p h j", j=PAGES)

            z_sb = Z[:, 0, :, :].rearrange("p h j -> p (h j)")
            z_fx = Z[:, 1, :, :].rearrange("p h j -> p (h j)")

            def weights(n, extract):
                dve.wait_ge(S["kused"], PAGES * (n + 1))
                own.step(dve.scalar_tensor_tensor(out=zx[:, :], in0=z_fx, scalar=SCALE,
                                                  in1=FB[:, bass.ds(n, 1), :].rearrange("p a f -> p (a f)"),
                                                  op0=ALU.mult, op1=ALU.add))
                dve.tensor_reduce(mxp[:, :], by_head(zx[:, :]), AX, ALU.max).then_inc(S["mx"], 1)
                own.step(dve.tensor_scalar(zr[:, :], z_sb, SCALE, 0.0, ALU.mult, ALU.max))
                dve.wait_ge(S["ssl"], n + 1)
                own.step(dve.tensor_tensor(sp_h[:, :, 1:PAGES + 1], by_head(zr[:, :]), by_head(zs[:, :]), ALU.add))
                flat = lambda x: x[:, :, :].rearrange("p h j -> p (h j)")
                dve.tensor_tensor_scan(flat(run), flat(seg), flat(sp_h), 0.0,
                                       ALU.mult, ALU.add).then_inc(S["ssp"], 1)
                dve.wait_ge(S["mxT"], n + 1)
                own.step(dve.tensor_reduce(m8[:, :], bank[4][0:H, 0:P], AX, ALU.max))
                dve.tensor_scalar(diag[:, :], ident[0:H, 0:H], m8[:, 0:1], None, ALU.mult).then_inc(S["diag"], 1)
                dve.wait_ge(S["C2"], n + 1)
                dve.scalar_tensor_tensor(out=ts[:, :], in0=z_sb, scalar=SCALE, in1=bank[5][:, 0:P],
                                         op0=ALU.mult, op1=ALU.subtract).then_inc(S["ts"], 1)
                dve.wait_ge(S["mb"], n + 1)
                mx = MX[:, bass.ds(n, 1), :].rearrange("p a h -> p (a h)")
                own.step(dve.tensor_copy(mx, bank[4][:, P:P + H]))
                dve.tensor_tensor(by_head(zx[:, :]), by_head(zx[:, :]), over(mx, PAGES), ALU.subtract).then_inc(S["zx"], 1)
                dve.wait_ge(S["w_fx"], n + 1)
                dve.tensor_reduce(dsum[:, :], PR[:, 1, :, 0:H].rearrange("p j h -> p h j"), AX, ALU.add).then_inc(S["dsum"], 1)
                if extract:
                    outputs(n - 1)
                dve.wait_ge(S["den"], n + 1)
                dve.tensor_copy(DEN[:, bass.ds(n, 1), :].rearrange("p a h -> p (a h)"), bank[5][:, 256:256 + H]).then_inc(S["denc"], 1)

            def outputs(b):
                dve.wait_ge(S["ext"], b + 1)
                own.step(dve.tensor_copy(qo[:, 0:H, bass.ds(SEQ + b, 1)].rearrange("p h a -> p (h a)"), bank[6][:, 0:H]))
                dve.tensor_copy(OF[:, bass.ds(b, 1), :].rearrange("p a h -> p (a h)"), bank[6][:, H:2 * H]).then_inc(S["extc"], 1)

            def row_copy(i, src, row, b):
                dve.wait_ge(S[f"tr{i}"], b + 1)
                dve.wait_ge(S[f"st{i}"], 32 * b)
                own.step(dve.tensor_copy(row[:, 0:2, :], src[:, 0:SEQ].rearrange("p (t d) -> p t d", d=HD)))
                dve.tensor_copy(row[0:NB, 2, :], src[0:NB, SEQ:384]).then_inc(S[f"row{i}"], 1)

            def turn(b, last):
                def diag_op(buf, mask, op):
                    for lo in (0, SEQ):
                        ins = dve.tensor_tensor(buf[:, lo:lo + P], buf[:, lo:lo + P], mask[:, :], op)
                        if lo == 0:
                            own.step(ins)
                    return ins

                if not last:
                    score(b + 1, 0)
                row_copy(0, bank[6], krow[0], b)
                row_copy(1, bank[7], vrow[0], b)
                if not last:
                    score(b + 1, 1)
                dve.wait_ge(S["sln"], b + 1)
                own.step(dve.tensor_scalar(pos_z[:, :], bank[6][:, 0:384], SCALE, 0.0, ALU.mult, ALU.max))
                own.step(dve.tensor_tensor(stay[:, :], stay[:, :], pos_z[:, :], ALU.add))
                diag_op(stay, tri_lt, ALU.mult).then_inc(S["sp"], 1)
                row_copy(2, bank[7], krow[1], b)
                row_copy(3, bank[4], vrow[1], b)
                dve.wait_ge(S["kv3"], b + 1)
                dve.tensor_tensor(QK[:, bass.ds(b, 1), :].rearrange("p a n -> p (a n)"), at(qo, b + H, SEQ, T), kT[1][:, SEQ:T],
                                  ALU.mult).then_inc(S["own_kv"], 1)
                dve.tensor_copy(VN[:, bass.ds(b, 1), :].rearrange("p a n -> p (a n)"), vT[1][:, SEQ:T]).then_inc(S["own_kv"], 1)
                if not last:
                    score(b + 1, 2)
                dve.wait_ge(S["C"], b + 1)
                own.step(dve.tensor_copy(pos_z[:, :], bank[7][:, 0:384]))
                own.step(dve.scalar_tensor_tensor(out=att[:, :], in0=bank[6][:, 0:384], scalar=SCALE, in1=pos_z[:, :],
                                                  op0=ALU.mult, op1=ALU.subtract))
                diag_op(att, neg_sb, ALU.add).then_inc(S["t"], 1)
                dve.wait_ge(S["fxz"], b + 1)
                own.step(dve.tensor_scalar(zf[:, :], bank[5][:, 0:384], SCALE, None, ALU.mult))
                own.step(diag_op(zf, neg_fx, ALU.add))
                own.step(dve.tensor_reduce(nmax[:, 0:1], zf[:, 0:P], AX, ALU.max, negate=True))
                dve.tensor_reduce(nmax[:, 1:2], zf[:, P:384], AX, ALU.max, negate=True).then_inc(S["zf"], 1)
                dve.wait_ge(S["fp"], 2 * b + 2)
                own.step(dve.reciprocal(rinv[:, :], rsum[:, :]))
                own.step(dve.tensor_scalar(pf[:, 0:P], pf[:, 0:P], rinv[:, 0:1], None, ALU.mult))
                dve.tensor_scalar(pf[:, P:384], pf[:, P:384], rinv[:, 1:2], None, ALU.mult).then_inc(S["pn"], 1)
                if last:
                    outputs(b)
                else:
                    score(b + 1, 3)
                    weights(b + 1, True)

            dve.wait_ge(S["pad"], 1)
            for q in range(4):
                score(0, q)
            weights(0, False)
            with dve.Fori(0, NB - 1) as b:
                own.enter(b, DVE_TURN)
                turn(b, False)
            own.leave(NB - 1)
            turn(NB - 1, True)
            idh = ident[0:NB, 0:NB].rearrange("b (h n) -> b h n", h=1).to_broadcast([NB, H, NB])
            dve.tensor_tensor(dlf[:, :, :], over(lf[0:NB, 2, :], NB), idh, ALU.mult).then_inc(S["lfd"], 1)
            dve.wait_ge(S["done1"], 1)

            def hb(x):
                return x[:, :].rearrange("p (h b) -> p h b", b=NB)

            mxv = MX[:, :, :].rearrange("p b h -> p h b")
            own_z, top, den, rec, num, num2 = fin
            dve.wait_ge(S["extc"], NB)
            dve.wait_ge(S["denc"], NB)
            own.step(dve.tensor_copy(top[:, :], bank[4][:, 64:128]))
            own.step(dve.scalar_tensor_tensor(out=own_z[:, :], in0=bank[4][:, 0:64], scalar=SCALE, in1=top[:, :],
                                              op0=ALU.mult, op1=ALU.subtract))
            own.step(dve.tensor_tensor(hb(top), mxv, hb(own_z), ALU.max))
            own.step(dve.tensor_tensor(ab[:, 0, :].rearrange("p (h b) -> p h b", b=NB), mxv, hb(top), ALU.subtract))
            dve.tensor_tensor(ab[:, 1, :], own_z[:, :], top[:, :], ALU.subtract).then_inc(S["done2"], 1)
            dve.wait_ge(S["done3"], 1)
            av = ab[:, 0, :].rearrange("p (h b) -> p h b", b=NB)
            own.step(dve.tensor_tensor(hb(den), DEN[:, :, :].rearrange("p b h -> p h b"), av, ALU.mult))
            own.step(dve.tensor_tensor(den[:, :], den[:, :], ab[:, 1, :], ALU.add))
            own.step(dve.reciprocal(rec[:, :], den[:, :]))
            own.step(dve.tensor_tensor(hb(num), OF[:, :, :].rearrange("p b h -> p h b"), av, ALU.mult))
            own.step(dve.tensor_tensor(num2[:, :], VN[:, :, :].rearrange("p h n -> p (h n)"), ab[:, 1, :], ALU.mult))
            own.step(dve.tensor_tensor(num[:, :], num[:, :], num2[:, :], ALU.add))
            own.step(dve.tensor_tensor(qo[:, H:2 * H, SEQ:T], hb(num), hb(rec), ALU.mult))
        bstack.close()
    done_with(nc, S)


G_FFN, G_GRP = 16, 32
ROUTE_BIG = 1.0e30


def ffn(nc, ctx, a, ident, ones, tri_lt, gcol, xT, xn, qo, wr, br, bank, sem, y_prompt, y_sample,
        u_rows, h_rows, y_rows):
    def sb(name, shape, dt=F32, where=ctx):
        return where.enter_context(nc.sbuf_tensor(name, shape, dt))

    idx = sb("idx", [P, PAIRS + 1], I32)
    place = sb("place", [P, 3, 2], I32)
    gates = sb("gates", [P, 3, 2])
    extra = sb("extra", [1, 2, EXTRA], I32)

    wctx = ExitStack()
    ws = sb("ws", [P, 6, KC * 256], where=wctx)
    SLOT = [4, 5, 0, 1, 2, 3]
    FIRST = [3, 3, 3, 3, 1, 1]
    W = [sem(f"w_slot{i}") for i in range(6)]
    w_gate = a["w_expert_gate"][0].rearrange("e (p c) f -> e p (c f)", p=P)
    w_up = a["w_expert_up"][0].rearrange("e (p c) f -> e p (c f)", p=P)
    w_down = a["w_expert_down"][0].rearrange("e (j p) d -> e p j d", p=P)
    w_out = a["w_out"][0].rearrange("(c p) n -> p c n", p=P)

    def load_expert(eng, k, e, cond=None):
        s = SLOT[k]
        more = {} if cond is None else {"cond": cond, "bounds_check": "skip_entire_dma"}
        if k % 3 == 2:
            dst = ws[:, s, :].rearrange("p (j d) -> p j d", j=2)
            src = w_down[bass.ds(e, 1)].rearrange("a p j d -> (a p) j d")
        else:
            dst = ws[:, s, :]
            src = (w_gate, w_up)[k % 3][bass.ds(e, 1)].rearrange("a p f -> (a p) f")
        eng.dma_start(dst, src, **more).then_inc(W[s], 16)

    cctx = ExitStack()
    rst = sb("c_rst", [P, 2, T], where=cctx)
    rstd = sb("c_rstd", [P, 2, T], where=cctx)
    stage = sb("stage", [P, 2, D], where=cctx)
    io32 = sb("io32", [P, P], I32, where=cctx)
    iota = sb("iota", [P, P], where=cctx)
    tok = sb("tok", [P, 3], where=cctx)
    toki = sb("toki", [P, 3], I32, where=cctx)
    valid = sb("valid", [P, 3], where=cctx)
    thr = sb("thr", [P, 4], where=cctx)
    lg = sb("lg", [P, 3, NG + NE], where=cctx)
    mask = sb("mask", [P, 3, NE], where=cctx)
    ext = sb("ext", [NE, P], where=cctx)
    ohs = sb("ohs", [P, 3, 2, P], where=cctx)
    ohb = sb("ohb", [P, 3, 2, PAIRS + 1], where=cctx)
    r2 = sb("r2", [P, 3, 5], where=cctx)
    gmx = sb("gmx", [P, 3], where=cctx)
    rg = sb("rg", [P, 3, NG], where=cctx)
    re_ = sb("re_", [P, 3, NE], where=cctx)
    tmp = sb("r_tmp", [P, 3, NE], where=cctx)
    oh = [sb(f"oh{k}", [P, 3, NE], where=cctx) for k in range(2)]
    gsel = sb("gsel", [P, 3, NG], where=cctx)
    top = [sb(f"top{k}", [P, 3], where=cctx) for k in range(2)]
    eid = sb("eid", [P, 3, 2], where=cctx)
    rank = sb("rank", [P, 3, 2], where=cctx)
    full = sb("full", [P, 3, 2], where=cctx)
    first = sb("first", [P, 3, 2], where=cctx)
    pre = sb("pre", [P, 3, 2], where=cctx)
    posn = sb("posn", [P, 3, 2], where=cctx)
    blk = sb("blk", [P, 3, 2], where=cctx)
    cmp6 = sb("cmp6", [P, 3, 2, 4], where=cctx)
    big = sb("big", [P, 3, 2, PAIRS + 1], where=cctx)
    small = sb("small", [P, 3, 2], where=cctx)
    cnt4 = sb("cnt4", [NE, 4, P], where=cctx)
    base = sb("base", [P, 2, NE], where=cctx)
    xb = sb("xb", [1, EXTRA, NE], where=cctx)
    xb2 = sb("xb2", [1, EXTRA, NE], where=cctx)
    xo = sb("xo", [1, 2, EXTRA], where=cctx)
    rks = sb("rks", [P, 3, NE], where=cctx)
    pthr = sb("pthr", [P, PAIRS + 2], where=cctx)
    C = {n: sem("c_" + n) for n in (
        "sq ss ms sqrt on o_done h sq2 ss2 ms2 sqrt2 un lgp rt rcopy rst0 rst1 iota ex "
        "mask cnt pe2 oh idxp idx act dve pool gg").split()}

    def mean_square(dve, out, ps, n, ms):
        dve.tensor_scalar(rst[:, out, :], ps, 1.0 / n, EPS, ALU.mult, ALU.add).then_inc(C[ms], 1)

    with nc.Block() as block:
        @block.sync
        def _(sp):
            load_expert(sp, 0, 0)
            load_expert(sp, 1, 0)
            for j in range(8):
                if j >= 4:
                    sp.wait_ge(C["o_done"], 2 * (j - 4) + 2)
                sp.dma_start(ws[:, j % 4, :].rearrange("p (c n) -> p c n", n=256),
                             w_out[:, :, j * 256:(j + 1) * 256]).then_inc(W[j % 4], 16)
            for k in range(2, 6):
                sp.wait_ge(C["o_done"], 2 * (4 + SLOT[k]) + 2)
                load_expert(sp, k, k // 3)

        @block.gpsimd
        def _(pool):
            own = Steps(pool, C["pool"])
            own.step(pool.iota(io32[:, :], [[1, P]], base=0, channel_multiplier=0))
            own.step(pool.tensor_copy(iota[:, :], io32[:, :]))
            own.step(pool.iota(toki[:, :], [[P, 3]], base=0, channel_multiplier=1))
            own.step(pool.tensor_copy(tok[:, :], toki[:, :]))
            own.step(pool.tensor_scalar(valid[:, :], tok[:, :], float(T), None, ALU.is_lt))
            own.step(pool.tensor_scalar(thr[:, :], iota[:, 0:4], float(SLOTS), float(SLOTS), ALU.mult, ALU.add))
            pool.memset(lg[:, :, :], 0.0).then_inc(C["iota"], 1)

        @block.tensor
        def _(pe):
            def column_sums(out, src, c0, n, done):
                for c in range(n):
                    mm = pe.matmul(out, ones[:, :], src[:, c0 + c, :], start=(c == 0), stop=(c == n - 1))
                mm.then_inc(C[done], 1)

            pe.wait_ge(C["sq"], 1)
            column_sums(bank[0][:, 0:T], xn, 0, H, "ss")
            column_sums(bank[1][:, 0:T], xn, H, H, "ss")
            pe.wait_ge(C["on"], 2 * H)
            with pe.Fori(0, 2) as r:
                pe.wait_ge(C["h"], 8 * r)
                for j in range(4):
                    pe.wait_ge(W[j], 16 * r + 16)
                    for m in range(2):
                        for c in range(KC):
                            mm = pe.matmul(bank[2 * j + m][:, 0:T], ws[:, j, c * 256 + m * P:c * 256 + (m + 1) * P],
                                           qo[:, c, :], start=(c == 0), stop=(c == KC - 1))
                        mm.then_inc(C["o_done"], 1)
            pe.wait_ge(C["sq2"], 1)
            column_sums(bank[0][:, 0:T], qo, 0, KC, "ss2")
            pe.wait_ge(C["un"], KC)
            for t, (lo, n) in enumerate(TILES):
                for c in range(KC):
                    mm = pe.matmul(bank[1][0:n, t * 36:(t + 1) * 36], xn[:, c, lo:lo + n], wr[:, c, :],
                                   start=(c == 0), stop=(c == KC - 1))
            mm.then_inc(C["lgp"], 1)
            i = 0
            for src in (xn, xT):
                for lo, n in TILES:
                    for k in range(4):
                        if i >= 4:
                            pe.wait_ge(C["rcopy"], i - 3)
                        for c in range(4):
                            mm = pe.transpose(bank[4 + k][0:n, c * P:(c + 1) * P], src[:, 4 * k + c, lo:lo + n], ident[:, :])
                        mm.then_inc(C["rt"], 1)
                        i += 1
            pe.wait_ge(C["mask"], 1)
            for t in range(3):
                out = bank[2][:, t * NE:(t + 1) * NE]
                for s in range(t):
                    pe.matmul(out, ones[:, :], mask[:, s, :], start=(s == 0), stop=False)
                mm = pe.matmul(out, tri_lt[:, :], mask[:, t, :], start=(t == 0), stop=True)
            for t in range(3):
                mm = pe.matmul(bank[3][0:NE, 0:P], mask[:, t, :], ones[:, :], start=(t == 0), stop=(t == 2))
            mm.then_inc(C["cnt"], 1)
            pe.wait_ge(C["ex"], 1)
            pe.matmul(bank[3][:, P:P + NE], ext[:, :], tri_lt[0:NE, 0:NE], start=True, stop=True)
            pe.matmul(bank[3][:, P + NE:P + 2 * NE], ext[:, :], ident[0:NE, 0:NE], start=True, stop=True).then_inc(C["pe2"], 1)
            pe.wait_ge(C["oh"], 1)
            for i in range(6):
                mm = pe.matmul(bank[0][:, 0:PAIRS + 1], ohs[:, i // 2, i % 2, :], ohb[:, i // 2, i % 2, :],
                               start=(i == 0), stop=(i == 5))
            mm.then_inc(C["idxp"], 1)

        @block.scalar
        def _(act):
            act.wait_ge(C["gg"], 1)
            nc.scalar.activation(xn[:, :, :].rearrange("p c t -> p (c t)"), qo[:, :, :].rearrange("p c t -> p (c t)"),
                                 ACT.Square).then_inc(C["sq"], 1)
            act.wait_ge(C["ms"], 2)
            nc.scalar.activation(rst[:, :, :], rst[:, :, :], ACT.Sqrt).then_inc(C["sqrt"], 1)
            act.wait_ge(C["h"], KC)
            nc.scalar.activation(qo[:, :, :].rearrange("p c t -> p (c t)"), xT[:, :, :].rearrange("p c t -> p (c t)"),
                                 ACT.Square).then_inc(C["sq2"], 1)
            act.wait_ge(C["ms2"], 1)
            nc.scalar.activation(rst[:, 0, :], rst[:, 0, :], ACT.Sqrt).then_inc(C["sqrt2"], 1)
            i = 0
            for dst in (u_rows, h_rows):
                for lo, n in TILES:
                    s = (i // 4) % 2
                    if i >= 8:
                        act.wait_ge(C[f"rst{s}"], 16 * (i // 8))
                    for k in range(4):
                        act.wait_ge(C["rt"], i + 1)
                        nc.scalar.activation(stage[0:n, s, k * 512:(k + 1) * 512], bank[4 + k][0:n, :], ACT.Copy).then_inc(C["rcopy"], 1)
                        i += 1
                    act.wait_ge(C["rcopy"], i)
                    act.dma_start(dst[lo:lo + n, :], stage[0:n, s, :]).then_inc(C[f"rst{s}"], 16)
            act.wait_ge(C["rst0"], 48)
            act.wait_ge(C["rst1"], 48)
            act.wait_ge(C["act"], 1)
            nc.scalar.activation(r2[:, :, :], r2[:, :, :], ACT.Exp).then_inc(C["gg"], 1)

        @block.vector
        def _(dve):
            own = Steps(dve, C["dve"])
            nc.vector.memset(r2[:, :, :], 0.0).then_inc(C["gg"], 1)
            dve.wait_ge(C["ss"], 2)
            for g in range(2):
                mean_square(dve, g, bank[g][:, 0:T], H * HD, "ms")
            dve.wait_ge(C["sqrt"], 1)
            own.step(dve.reciprocal(rstd[:, :, :], rst[:, :, :]))
            for c in range(2 * H):
                dve.scalar_tensor_tensor(out=qo[:, c, :], in0=qo[:, c, :], scalar=gcol[:, G_GRP + c:G_GRP + c + 1],
                                         in1=rstd[:, c // H, :], op0=ALU.mult, op1=ALU.mult).then_inc(C["on"], 1)
            with dve.Fori(0, 2) as r:
                for i in range(8):
                    dve.wait_ge(C["o_done"], 8 * r + i + 1)
                    dve.tensor_tensor(at(xT, 8 * r + i, 0, T), at(xT, 8 * r + i, 0, T), bank[i][:, 0:T],
                                      ALU.add).then_inc(C["h"], 1)
            dve.wait_ge(C["ss2"], 1)
            mean_square(dve, 0, bank[0][:, 0:T], D, "ms2")
            dve.wait_ge(C["sqrt2"], 1)
            own.step(dve.reciprocal(rstd[:, 0, :], rst[:, 0, :]))
            for c in range(KC):
                dve.scalar_tensor_tensor(out=xn[:, c, :], in0=xT[:, c, :], scalar=gcol[:, G_FFN + c:G_FFN + c + 1],
                                         in1=rstd[:, 0, :], op0=ALU.mult, op1=ALU.mult).then_inc(C["un"], 1)
            dve.wait_ge(C["iota"], 1)
            dve.wait_ge(C["lgp"], 1)

            def tt(out, x, y, op):
                own.step(dve.tensor_tensor(out, x, y, op))

            def ts(out, x, s1, s2, op0, op1=ALU.bypass):
                own.step(dve.tensor_scalar(out, x, s1, s2, op0, op1) if s2 is not None else dve.tensor_scalar(out, x, s1, None, op0))

            def red(out, x, op):
                own.step(dve.tensor_reduce(out, x, AX, op))

            brv = br[:, :].rearrange("p (t e) -> p t e", t=1)
            tt(lg[:, 0:2, :], bank[1][:, 0:72].rearrange("p (t e) -> p t e", e=36), brv.to_broadcast([P, 2, 36]), ALU.add)
            tt(lg[0:NB, 2, :], bank[1][0:NB, 72:108], br[0:NB, :], ALU.add)
            iota4 = iota[:, 0:NG].rearrange("p (t e) -> p t e", t=1).to_broadcast([P, 3, NG])
            iota32 = iota[:, 0:NE].rearrange("p (t e) -> p t e", t=1).to_broadcast([P, 3, NE])

            def first_max(x, n, numbers, best, hot, scratch, number):
                red(best, x, ALU.max)
                tt(scratch, x, over(best, n), ALU.is_lt)
                ts(scratch, scratch, 1.0e4, None, ALU.mult)
                tt(scratch, scratch, numbers, ALU.add)
                red(number, scratch, ALU.min)
                tt(hot, numbers, over(number, n), ALU.is_equal)

            first_max(lg[:, :, 0:NG], NG, iota4, gmx[:, :], gsel[:, :, :], rg[:, :, :], top[0][:, :])
            tt(r2[:, :, 0:NG], lg[:, :, 0:NG], over(gmx[:, :], NG), ALU.subtract)
            ts(re_[:, :, :].rearrange("p t (g e) -> p (t g) e", g=NG),
               over(gsel[:, :, :].rearrange("p t g -> p (t g)"), EPG), -1.0, ROUTE_BIG, ALU.add, ALU.mult)
            tt(re_[:, :, :], re_[:, :, :], lg[:, :, NG:NG + NE], ALU.add)
            first_max(re_[:, :, :], NE, iota32, top[0][:, :], oh[0][:, :, :], tmp[:, :, :], eid[:, :, 0])
            ts(tmp[:, :, :], oh[0][:, :, :], -2.0 * ROUTE_BIG, None, ALU.mult)
            tt(re_[:, :, :], re_[:, :, :], tmp[:, :, :], ALU.add)
            first_max(re_[:, :, :], NE, iota32, top[1][:, :], oh[1][:, :, :], tmp[:, :, :], eid[:, :, 1])
            dve.tensor_tensor(r2[:, :, NG], top[1][:, :], top[0][:, :], ALU.subtract).then_inc(C["act"], 1)
            tt(mask[:, :, :], oh[0][:, :, :], oh[1][:, :, :], ALU.add)
            dve.tensor_tensor(mask[:, :, :], mask[:, :, :], over(valid[:, :], NE), ALU.mult).then_inc(C["mask"], 1)
            dve.wait_ge(C["cnt"], 1)
            for j in range(4):
                ts(cnt4[:, j, :], bank[3][0:NE, 0:P], float(SLOTS * (j + 1)), None, ALU.is_gt)
            own.step(dve.tensor_reduce(ext[:, :], cnt4[:, :, :].rearrange("e j p -> e p j"), AX, ALU.add))
            dve.tensor_copy(rks[:, :, :].rearrange("p t e -> p (t e)"), bank[2][:, 0:3 * NE]).then_inc(C["ex"], 1)
            dve.wait_ge(C["pe2"], 1)
            own.step(dve.tensor_copy(base[:, :, :].rearrange("p a e -> p (a e)"), bank[3][:, P:P + 2 * NE]))
            b0 = base[:, 0, :].rearrange("p (t e) -> p t e", t=1).to_broadcast([P, 3, NE])
            for k in range(2):
                tt(tmp[:, :, :], oh[k][:, :, :], rks[:, :, :], ALU.mult)
                red(rank[:, :, k], tmp[:, :, :], ALU.add)
                tt(tmp[:, :, :], oh[k][:, :, :], b0, ALU.mult)
                red(pre[:, :, k], tmp[:, :, :], ALU.add)
            flat = lambda x: x.rearrange("p t k -> p (t k)")
            tt(cmp6[:, :, :, :].rearrange("p t k j -> p (t k) j"), over(flat(rank[:, :, :]), 4),
               thr[:, :].rearrange("p (a j) -> p a j", a=1).to_broadcast([P, 6, 4]), ALU.is_ge)
            red(flat(full[:, :, :]), cmp6[:, :, :, :].rearrange("p t k j -> p (t k) j"), ALU.add)
            ts(flat(first[:, :, :]), flat(full[:, :, :]), 0.0, None, ALU.is_equal)
            tt(flat(blk[:, :, :]), flat(pre[:, :, :]), flat(full[:, :, :]), ALU.add)
            ts(flat(blk[:, :, :]), flat(blk[:, :, :]), float(NE - 1), None, ALU.add)
            tt(flat(small[:, :, :]), flat(eid[:, :, :]), flat(blk[:, :, :]), ALU.subtract)
            tt(flat(small[:, :, :]), flat(small[:, :, :]), flat(first[:, :, :]), ALU.mult)
            tt(flat(blk[:, :, :]), flat(blk[:, :, :]), flat(small[:, :, :]), ALU.add)
            tt(flat(blk[:, :, :]), flat(blk[:, :, :]), flat(full[:, :, :]), ALU.subtract)
            ts(flat(posn[:, :, :]), flat(blk[:, :, :]), float(SLOTS), None, ALU.mult)
            tt(flat(posn[:, :, :]), flat(posn[:, :, :]), flat(rank[:, :, :]), ALU.add)
            own.step(dve.tensor_copy(place[:, :, :], posn[:, :, :]))
            ts(pthr[:, :], iota[:, 0:PAIRS + 2], float(P), None, ALU.mult)
            thr_lo = pthr[:, 0:PAIRS + 1].rearrange("p (a j) -> p a j", a=1).to_broadcast([P, 6, PAIRS + 1])
            thr_hi = pthr[:, 1:PAIRS + 2].rearrange("p (a j) -> p a j", a=1).to_broadcast([P, 6, PAIRS + 1])
            pv = over(flat(posn[:, :, :]), PAIRS + 1)
            bigv = big[:, :, :, :].rearrange("p t k j -> p (t k) j")
            ohbv = ohb[:, :, :, :].rearrange("p t k j -> p (t k) j")
            tt(ohbv, pv, thr_lo, ALU.is_ge)
            tt(bigv, pv, thr_hi, ALU.is_ge)
            red(flat(full[:, :, :]), bigv, ALU.add)
            tt(ohbv, ohbv, bigv, ALU.subtract)
            ts(flat(full[:, :, :]), flat(full[:, :, :]), float(P), None, ALU.mult)
            tt(flat(full[:, :, :]), flat(posn[:, :, :]), flat(full[:, :, :]), ALU.subtract)
            for t in range(3):
                ts(ohb[:, t, :, :], ohb[:, t, :, :], tok[:, t:t + 1], valid[:, t:t + 1], ALU.mult, ALU.mult)
            for t in range(3):
                for k in range(2):
                    ts(ohs[:, t, k, :], iota[:, :], full[:, t, k:k + 1], None, ALU.is_equal)
            io8 = iota[0:1, 0:EXTRA].rearrange("p (b e) -> p b e", e=1).to_broadcast([1, EXTRA, NE])
            be = base[0:1, 0, :].rearrange("p (b e) -> p b e", b=1).to_broadcast([1, EXTRA, NE])
            ce = base[0:1, 1, :].rearrange("p (b e) -> p b e", b=1).to_broadcast([1, EXTRA, NE])
            tt(xb[:, :, :], io8, be, ALU.subtract)
            tt(xb2[:, :, :], xb[:, :, :], ce, ALU.is_lt)
            ts(xb[:, :, :], xb[:, :, :], 0.0, None, ALU.is_ge)
            tt(xb[:, :, :], xb[:, :, :], xb2[:, :, :], ALU.mult)
            red(xo[:, 1, :], xb[:, :, :], ALU.add)
            tt(xb[:, :, :], xb[:, :, :], iota[0:1, 0:NE].rearrange("p (b e) -> p b e", b=1).to_broadcast([1, EXTRA, NE]), ALU.mult)
            red(xo[:, 0, :], xb[:, :, :], ALU.add)
            dve.tensor_copy(extra[:, :, :], xo[:, :, :]).then_inc(C["oh"], 1)
            dve.wait_ge(C["gg"], 2)
            red(gmx[:, :], r2[:, :, 0:NG], ALU.add)
            own.step(dve.reciprocal(gmx[:, :], gmx[:, :]))
            ts(top[0][:, :], r2[:, :, NG], 1.0, None, ALU.add)
            own.step(dve.reciprocal(top[0][:, :], top[0][:, :]))
            tt(gates[:, :, 0], top[0][:, :], gmx[:, :], ALU.mult)
            tt(gates[:, :, 1], gates[:, :, 0], r2[:, :, NG], ALU.mult)
            dve.wait_ge(C["idxp"], 1)
            own.step(dve.tensor_copy(idx[:, :], bank[0][:, 0:PAIRS + 1]))
    cctx.close()
    done_with(nc, C)

    dctx = ExitStack()
    xg = sb("xg", [P, D], where=dctx)
    xgT = sb("xgT", [P, KC, P], where=dctx)
    gu = [sb(f"gu{k}", [P, 256], where=dctx) for k in range(2)]
    si = [sb(f"si{k}", [P, 2, SLOTS], where=dctx) for k in range(2)]
    hT = [sb(f"hT{k}", [P, 2, SLOTS], where=dctx) for k in range(2)]
    ys = [sb(f"ys{k}", [P, 1024], where=dctx) for k in range(2)]
    E = {n: sem("d_" + n) for n in (
        "xg xgp xgT gu0 gu1 guc0 guc1 t0 t1 si0 si1 h0 h1 y0 y1 yc0 yc1 yst0 yst1").split()}
    yv = y_rows.rearrange("(n s) d -> n s d", s=SLOTS)
    EXP_PAIRS = NE // 2

    with nc.Block() as block:
        @block.sync
        def _(sp):
            def free(k, n):
                sp.wait_ge(E[f"gu{k // 3}"] if k % 3 < 2 else E[f"y{k // 3}"], n)

            with sp.Fori(1, EXP_PAIRS) as n:
                for k in range(6):
                    free(k, n)
                    load_expert(sp, k, 2 * n + k // 3)
            with sp.Fori(EXP_PAIRS, PAIRS) as n:
                for blk_ in range(2):
                    i = (n - EXP_PAIRS) * 2 + blk_
                    e = sp.value_load(extra[0:1, 0, bass.ds(i, 1)], min_val=0, max_val=NE - 1)
                    used = sp.value_load(extra[0:1, 1, bass.ds(i, 1)], min_val=0, max_val=1)
                    for k in range(3 * blk_, 3 * blk_ + 3):
                        free(k, n)
                        load_expert(sp, k, e, used)

        @block.gpsimd
        def _(pool):
            for n in range(PAIRS + 1):
                if n:
                    pool.wait_ge(E["xgp"], 4 * n)
                pool.indirect_dma_start(xg[:, :], None, u_rows,
                                        bass.IndirectOffsetOnAxis(ap=idx[:, n:n + 1], axis=0)).then_inc(E["xg"], 16)
            pool.wait_ge(E["xg"], 16 * (PAIRS + 1))

        @block.tensor
        def _(pe):
            def tokens(n):
                pe.wait_ge(E["xg"], 16 * n + 16)
                xv = xg[:, :].rearrange("s (p c) -> s c p", c=KC)
                for k in range(4):
                    for c in range(4):
                        mm = pe.transpose(bank[4 + k][:, c * P:(c + 1) * P], xv[:, 4 * k + c, :], ident[:, :])
                    mm.then_inc(E["xgp"], 1)

            def gate_up(k, n):
                wg, wu = SLOT[3 * k], SLOT[3 * k + 1]
                pe.wait_ge(W[wg], 16 * (n + FIRST[wg]))
                pe.wait_ge(W[wu], 16 * (n + FIRST[wu]))
                for c in range(KC):
                    lhs = xgT[:, c, k * SLOTS:(k + 1) * SLOTS]
                    pe.matmul(bank[2 * k][0:SLOTS, 0:256], lhs, ws[:, wg, c * 256:(c + 1) * 256],
                              start=(c == 0), stop=(c == KC - 1))
                    mm = pe.matmul(bank[2 * k][SLOTS:P, 0:256], lhs, ws[:, wu, c * 256:(c + 1) * 256],
                                   start=(c == 0), stop=(c == KC - 1))
                mm.then_inc(E[f"gu{k}"], 1)

            def turn_over(k, n):
                pe.wait_ge(E[f"guc{k}"], n + 1)
                for j in range(2):
                    mm = pe.transpose(bank[2 * k + 1][:, j * P:(j + 1) * P], gu[k][:, j * P:(j + 1) * P], ident[:, :])
                mm.then_inc(E[f"t{k}"], 1)

            def down(k, n):
                wd = SLOT[3 * k + 2]
                pe.wait_ge(W[wd], 16 * (n + FIRST[wd]))
                pe.wait_ge(E[f"h{k}"], n + 1)
                for dc in range(2):
                    for j in range(2):
                        for dh in range(2):
                            d0 = j * D + dh * 1024 + dc * 512
                            mm = pe.matmul(bank[4 + 2 * k + dc][dh * SLOTS:(dh + 1) * SLOTS, :], hT[k][:, j, :],
                                           ws[:, wd, d0:d0 + 512], start=(j == 0), stop=(j == 1))
                mm.then_inc(E[f"y{k}"], 1)

            tokens(0)
            with pe.Fori(0, PAIRS) as n:
                pe.wait_ge(E["xgT"], 4 * n + 4)
                gate_up(0, n)
                gate_up(1, n)
                turn_over(0, n)
                pe.wait_ge(E["yc0"], 2 * n)
                pe.wait_ge(E["yc1"], 2 * n)
                tokens(n + 1)
                turn_over(1, n)
                pe.wait_ge(E["xgT"], 4 * n + 8)
                down(0, n)
                down(1, n)

        @block.scalar
        def _(act):
            def tokens(n, free):
                if free:
                    act.wait_ge(E["gu1"], n)
                for k in range(4):
                    act.wait_ge(E["xgp"], 4 * n + k + 1)
                    nc.scalar.activation(xgT[:, 4 * k:4 * k + 4, :].rearrange("p c s -> p (c s)"), bank[4 + k][:, :],
                                         ACT.Copy).then_inc(E["xgT"], 1)

            def silu(k, n):
                act.wait_ge(E[f"t{k}"], n + 1)
                act.wait_ge(E[f"h{k}"], n)
                gv = bank[2 * k + 1][:, 0:256].rearrange("p (j s) -> p j s", j=2)
                nc.scalar.activation(si[k][:, :, :], gv[:, :, 0:SLOTS], ACT.Silu).then_inc(E[f"si{k}"], 1)

            def store(k, n):
                for half in range(2):
                    act.dma_start(yv[bass.ds(2 * n + k, 1), :, half * 1024:(half + 1) * 1024].rearrange("a s d -> (a s) d"),
                                  ys[k][half * SLOTS:(half + 1) * SLOTS, :]).then_inc(E[f"yst{k}"], 16)

            tokens(0, False)
            with act.Fori(0, PAIRS) as n:
                silu(0, n)
                tokens(n + 1, True)
                silu(1, n)
                act.wait_ge(E["yc0"], 2 * n + 2)
                store(0, n)
                act.wait_ge(E["y1"], n + 1)
                act.wait_ge(E["yst1"], 32 * n)
                for i in range(2):
                    nc.scalar.activation(ys[1][:, i * 512:(i + 1) * 512], bank[6 + i][:, :], ACT.Copy).then_inc(E["yc1"], 1)
                act.wait_ge(E["yc1"], 2 * n + 2)
                store(1, n)
            act.wait_ge(E["yst0"], 32 * PAIRS)
            act.wait_ge(E["yst1"], 32 * PAIRS)

        @block.vector
        def _(dve):
            with dve.Fori(0, PAIRS) as n:
                for k in range(2):
                    dve.wait_ge(E[f"gu{k}"], n + 1)
                    dve.wait_ge(E[f"t{k}"], n)
                    dve.tensor_copy(gu[k][:, :], bank[2 * k][:, 0:256]).then_inc(E[f"guc{k}"], 1)
                for k in range(2):
                    dve.wait_ge(E[f"si{k}"], n + 1)
                    dve.wait_ge(E[f"y{k}"], n)
                    uv = bank[2 * k + 1][:, 0:256].rearrange("p (j s) -> p j s", j=2)
                    dve.tensor_tensor(hT[k][:, :, :], si[k][:, :, :], uv[:, :, SLOTS:P], ALU.mult).then_inc(E[f"h{k}"], 1)
                dve.wait_ge(E["y0"], n + 1)
                dve.wait_ge(E["yst0"], 32 * n)
                for i in range(2):
                    dve.tensor_copy(ys[0][:, i * 512:(i + 1) * 512], bank[4 + i][:, :]).then_inc(E["yc0"], 1)
    dctx.close()
    wctx.close()

    with ExitStack() as ectx:
        gf = sb("gf", [P, D], where=ectx)
        hr = sb("hr", [P, 3, D], where=ectx)
        yr = sb("yr", [P, 3, 2, D], where=ectx)
        junk = sb("junk", [P, D], where=ectx)
        ssq = sb("ssq", [P, 3], where=ectx)
        rms = sb("rms", [P, 3], where=ectx)
        F = {n: sem("e_" + n) for n in "gf h0 h1 h2 g00 g01 g10 g11 g20 g21 sum sq ms sqrt out st dve".split()}
        with nc.Block() as block:
            @block.sync
            def _(sp):
                for t, (lo, n) in enumerate(TILES):
                    sp.dma_start(hr[0:n, t, :], h_rows[lo:lo + n, :]).then_inc(F[f"h{t}"], 16)
                sp.dma_start(gf[:, :], a["norm_final_g"].rearrange("(a d) -> a d", a=1).to_broadcast([P, D])).then_inc(F["gf"], 16)
                for t, (lo, n) in enumerate(TILES):
                    sp.wait_ge(F["out"], t + 1)
                    dst = y_prompt[0, lo:lo + n] if t < 2 else y_sample.rearrange("b s d -> (b s) d")
                    sp.dma_start(dst, hr[0:n, t, :]).then_inc(F["st"], 16)
                sp.wait_ge(F["st"], 48)

            @block.gpsimd
            def _(pool):
                for t, (lo, n) in enumerate(TILES):
                    for k in range(2):
                        pool.indirect_dma_start(yr[0:n, t, k, :], None, y_rows,
                                                bass.IndirectOffsetOnAxis(ap=place[0:n, t, k:k + 1], axis=0)).then_inc(F[f"g{t}{k}"], 16)

            @block.scalar
            def _(act):
                for t, (lo, n) in enumerate(TILES):
                    act.wait_ge(F["sum"], t + 1)
                    if t:
                        act.wait_ge(F["sq"], t)
                    nc.scalar.activation(junk[0:n, :], hr[0:n, t, :], ACT.Square, accum_out=ssq[0:n, t:t + 1]).then_inc(F["sq"], 1)
                    act.wait_ge(F["ms"], t + 1)
                    nc.scalar.activation(rms[0:n, t:t + 1], rms[0:n, t:t + 1], ACT.Sqrt).then_inc(F["sqrt"], 1)

            @block.vector
            def _(dve):
                own = Steps(dve, F["dve"])
                dve.wait_ge(F["gf"], 16)
                for t, (lo, n) in enumerate(TILES):
                    dve.wait_ge(F[f"h{t}"], 16)
                    for k in range(2):
                        dve.wait_ge(F[f"g{t}{k}"], 16)
                        ins = dve.scalar_tensor_tensor(out=hr[0:n, t, :], in0=yr[0:n, t, k, :], scalar=gates[0:n, t, k:k + 1],
                                                       in1=hr[0:n, t, :], op0=ALU.mult, op1=ALU.add)
                        if k == 0:
                            own.step(ins)
                        else:
                            ins.then_inc(F["sum"], 1)
                    dve.wait_ge(F["sq"], t + 1)
                    dve.tensor_scalar(rms[0:n, t:t + 1], ssq[0:n, t:t + 1], 1.0 / D, EPS, ALU.mult, ALU.add).then_inc(F["ms"], 1)
                    dve.wait_ge(F["sqrt"], t + 1)
                    own.step(dve.reciprocal(ssq[0:n, t:t + 1], rms[0:n, t:t + 1]))
                    dve.scalar_tensor_tensor(out=hr[0:n, t, :], in0=hr[0:n, t, :], scalar=ssq[0:n, t:t + 1],
                                             in1=gf[0:n, :], op0=ALU.mult, op1=ALU.mult).then_inc(F["out"], 1)


_INS = ["x_prompt", "x_sample", "cache_sb_k", "cache_sb_v", "cache_fox_k", "cache_fox_v", "cache_fox_logf",
        "norm_attn_g", "w_in", "b_forget", "g_sb_out", "g_fox_out", "w_out", "norm_ffn_g", "w_router_group",
        "b_router_group", "w_router_expert", "b_router_expert", "w_expert_gate", "w_expert_up", "w_expert_down",
        "norm_final_g"]
_KV_P, _KV_S = (1, 1, SEQ, H, HD), (1, NB, 1, H, HD)
_OUTS = [(1, SEQ, D), (NB, 1, D), _KV_P, _KV_P, _KV_P, _KV_P, (1, 1, SEQ, H), _KV_S, _KV_S, _KV_S, _KV_S, (1, NB, 1, H)]


def kernel(**inputs):
    import numpy as _np
    import concourse.bacc as _bacc
    from concourse.bass_utils import run_bass_kernel_spmd as _run

    nc = _bacc.Bacc("TRN2", target_bir_lowering=False, num_devices=1)
    arrays, a = {}, {}
    data = {name: _np.ascontiguousarray(inputs[name]) for name in _INS}
    data["pages"] = _np.ascontiguousarray(inputs["page_table"][:, ::-1]).reshape(1, NB * PAGES)
    for name, x in data.items():
        arrays[f"in_{name}"] = x
        a[name] = nc.dram_tensor(f"in_{name}", x.shape, mybir.dt.from_np(x.dtype), kind="ExternalInput").ap()
    outs = [nc.dram_tensor(f"out_{i}", shape, F32, kind="ExternalOutput").ap() for i, shape in enumerate(_OUTS)]
    u_rows = nc.dram_tensor("u_rows", (T, D), F32).ap()
    h_rows = nc.dram_tensor("h_rows", (T, D), F32).ap()
    y_rows = nc.dram_tensor("y_rows", (BLOCKS * SLOTS, D), F32).ap()
    hybrid_step(nc, a, outs, u_rows, h_rows, y_rows)
    r = _run(nc, [arrays], core_ids=[0])
    return tuple(r.results[0][f"out_{i}"] for i in range(len(_OUTS)))
```

```python
from contextlib import ExitStack

import concourse.bass as bass
from concourse import mybir

F32 = mybir.dt.float32
I32 = mybir.dt.int32
ALU = mybir.AluOpType
ACT = mybir.ActivationFunctionType
AX = mybir.AxisListType.X

P = 128
D = 2048
SEQ = 256
NB = 8
T = SEQ + NB
HD = 128
H = 8
KC = D // P
PAGES = 16
SCALE = HD ** -0.5
EPS = 1e-6
NG = 4
EPG = 8
NE = NG * EPG
FE = D // 8
SLOTS = 64
EXTRA = 8
BLOCKS = NE + EXTRA
PAIRS = BLOCKS // 2
NEG = -1.0e30
TILES = [(0, P), (P, P), (SEQ, NB)]
B_SEMS = ("k0 k1 k2 k3 v0 v1 v2 v3 kused vused w0 w1 pad "
          "sel bcast qb proj0 proj1 proj2 proj3 kv0 kv1 kv2 kv3 tr0 tr1 tr2 tr3 row0 row1 row2 row3 "
          "st0 st1 st2 st3 qf cm sbz sln sp C t at fxz zf fp pn sbo sboc tp pT fxo fxoc own_kv "
          "mx ssl ssp mxT diag mb zx C2 ts w_fx w_sb dsum osum ext extc den denc done1 done2 done3 "
          "dve act pool lfd")


class Steps:

    def __init__(self, eng, sem):
        self.eng, self.sem, self.base, self.n = eng, sem, 0, 0

    def step(self, ins):
        self.n += 1
        ins.then_inc(self.sem, 1)
        self.eng.wait_ge(self.sem, self.base + self.n)

    def enter(self, i, first, per_turn):
        self.start = self.base + self.n
        self.base, self.n, self.per_turn = self.start - first * per_turn + i * per_turn, 0, per_turn

    def leave(self, turns):
        assert self.n == self.per_turn, f"steps in a turn: {self.n}, not {self.per_turn}"
        self.base, self.n = self.start + turns * self.per_turn, 0


def wait_past(eng, sem, value):
    if not isinstance(value, int) or value > 0:
        eng.wait_ge(sem, value)


def done_with(nc, sems):
    nc.clear_and_free_semaphores(list(sems.values()))
    nc.all_engine_barrier()


def at(buf, i, lo, hi):
    return buf[:, bass.ds(i, 1), lo:hi].rearrange("p a f -> p (a f)")


def over(ap, n):
    s = list(ap.shape)
    return ap.rearrange("p (a o) -> p a o", o=1).to_broadcast([s[0], s[1], n])


def load_keys(sp, S, kring, caches, ptr, g, n_phys):
    for u in range(4):
        wait_past(sp, S["kused"], 4 * (g - 1) + u + 1 if not isinstance(g, int) or g else 0)
        page = sp.value_load(ptr[0:1, bass.ds(4 * g + u, 1)], min_val=0, max_val=n_phys - 1)
        for k in range(2):
            sp.dma_start(kring[:, u, k, :], caches[k][bass.ds(page, 1)].rearrange("a p f -> (a p) f")).then_inc(S[f"k{u}"], 16)


def score(dve, S, kring, qb, Z, n, q):
    if q == 0:
        dve.wait_ge(S["qb"], 4 * (n + 1))
    for u in range(4):
        dve.wait_ge(S[f"k{u}"], 32 * (4 * n + q + 1))
        for g in range(2):
            for h in range(H):
                k = kring[:, u, g, h * HD:(h + 1) * HD]
                ins = dve.tensor_tensor_reduce(k, k, qb[:, (g * H + h) * HD:(g * H + h + 1) * HD], 1.0, 0.0,
                                               ALU.mult, ALU.add, Z[:, g, h, 4 * q + u:4 * q + u + 1])
        ins.then_inc(S["kused"], 1)


def broadcast_queries(pe, S, banks, sel, qpart, n):
    pe.wait_ge(S["sel"], n + 1)
    for i in range(4):
        mm = pe.matmul(banks[i][:, :], sel[:, :], qpart[:, i * 512:(i + 1) * 512], start=True, stop=True)
    mm.then_inc(S["bcast"], 1)


def copy_queries(nc, act, S, banks, qb, n):
    act.wait_ge(S["bcast"], n + 1)
    for i in range(4):
        nc.scalar.activation(qb[:, i * 512:(i + 1) * 512], banks[i][:, :], ACT.Copy).then_inc(S["qb"], 1)


SLOT = [4, 5, 0, 1, 2, 3]
FIRST = [3, 3, 3, 3, 1, 1]


def load_expert(eng, a, ws, W, k, e):
    s = SLOT[k]
    if k % 3 == 2:
        dst = ws[:, s, :].rearrange("p (j d) -> p j d", j=2)
        src = a["w_expert_down"][0].rearrange("e (j p) d -> e p j d", p=P)[bass.ds(e, 1)].rearrange("a p j d -> (a p) j d")
    else:
        dst = ws[:, s, :]
        w = a["w_expert_gate" if k % 3 == 0 else "w_expert_up"][0].rearrange("e (p c) f -> e p (c f)", p=P)
        src = w[bass.ds(e, 1)].rearrange("a p f -> (a p) f")
    eng.dma_start(dst, src).then_inc(W[s], 16)


def load_out(eng, a, ws, W, j):
    w_out = a["w_out"][0].rearrange("(c p) n -> p c n", p=P)
    eng.dma_start(ws[:, j % 4, :].rearrange("p (c n) -> p c n", n=256),
                  w_out[:, :, j * 256:(j + 1) * 256]).then_inc(W[j % 4], 16)


def hybrid_step(nc, a, outs, u_rows, y_rows):
    (y_prompt, y_sample, sbk_p, sbv_p, fxk_p, fxv_p, logf_p, sbk_s, sbv_s, fxk_s, fxv_s, logf_s) = outs
    ctx = ExitStack()
    with ctx:
        def sem(name):
            return nc.alloc_semaphore(name=name)

        def sb(name, shape, dt=F32, where=ctx):
            return where.enter_context(nc.sbuf_tensor(name, shape, dt))

        bank = [ctx.enter_context(nc.psum_tensor(f"bank{i}", [P, 512], F32)) for i in range(8)]

        ident = sb("ident", [P, P])
        ones = sb("ones", [P, P])
        tri_ge = sb("tri_ge", [P, P])
        tri_gt = sb("tri_gt", [P, P])
        tri_le = sb("tri_le", [P, P])
        tri_lt = sb("tri_lt", [P, P])
        neg_sb = sb("neg_sb", [P, P])
        neg_fx = sb("neg_fx", [P, P])
        later = sb("later", [P, P])
        pick4 = sb("pick4", [P, 4, H])
        pick = sb("pick", [P, H])
        lastq4 = sb("lastq4", [P, 4, NB])
        lastq = sb("lastq", [P, NB + 1])
        seg = sb("seg", [P, H, PAGES + 1])
        gcol = sb("gcol", [P, 48])
        G_ATTN, G_FFN, G_GRP = 0, 16, 32
        xT = sb("xT", [P, KC, T])
        xn = sb("xn", [P, KC, T])
        qo = sb("qo", [P, 2 * H, T])
        lf = sb("lf", [P, 3, H])
        wr = sb("wr", [P, KC, 64])
        br = sb("br", [P, NG + NE])

        ws = sb("ws", [P, 6, KC * 256])
        W = [sem(f"w_slot{i}") for i in range(6)]

        s_const = sem("s_const")

        bctx = ExitStack()
        ctx.enter_context(bctx)
        qpart = sb("qpart", [P, 2 * H * HD], where=bctx)
        cTs = sb("cTs", [H, SEQ], where=bctx)
        FB = sb("FB", [P, NB, H * PAGES], where=bctx)
        ptr = sb("ptr", [1, NB * PAGES], I32, where=bctx)
        kring = ws[:, 0:2, :].rearrange("p s (a g f) -> p (s a) g f", a=2, g=2)
        qb = sb("qb", [P, 2 * H * HD], where=bctx)
        sel = sb("sel", [P, P], where=bctx)
        Z = sb("Z", [P, 2, H, PAGES], where=bctx)
        S = {n: sem("b_" + n) for n in B_SEMS.split()}
        n_phys = a["cache_sb_k"].shape[1]
        key_caches = [a[n][0].rearrange("n p h d -> n p (h d)") for n in ("cache_sb_k", "cache_fox_k")]

        actx = ExitStack()
        xrow = kring[:, 0:3, :, :].rearrange("p u g f -> p u (g f)")
        wq = ws[:, 2:6, :].rearrange("p s (c n) -> p s c n", c=KC)
        grow = sb("grow", [48, P], where=actx)
        ptc = sb("ptc", [P, 1], I32, where=actx)
        wf = sb("wf", [P, KC, 32], where=actx)
        fpart = sb("fpart", [P, T], where=actx)
        bf = sb("bf", [P, H], where=actx)
        rst = sb("rst", [P, T], where=actx)
        rstd = sb("rstd", [P, T], where=actx)
        fl = sb("fl", [P, 3 * H], where=actx)
        fa = sb("fa", [P, 3 * H], where=actx)
        fr = sb("fr", [P, 3 * H], where=actx)
        lfr = sb("lfr", [P, P * H], where=actx)
        LFT = sb("LFT", [P, H * P], where=actx)
        ltot = sb("ltot", [P, H], where=actx)
        totb = sb("totb", [P, H, P], where=actx)

        A = {n: sem("a_" + n) for n in (
            "x0 x1 x2 g_in pt_in ptc_in wf_in bf_in wr_in tpose tcopy gt sq ss ms sqrt xn fp fpc f fl fln "
            "lf q_done q_evac qp qpc lft ltc tot ct ctc fb fbc lfg lst w0 w1 w2 w3 pool dve act").split()}
        w_in = a["w_in"][0].rearrange("(c p) n -> p c n", p=P)

        with nc.Block() as block:
            @block.sync
            def _(sp):
                for t, (lo, n) in enumerate(TILES):
                    src = a["x_prompt"][0, lo:lo + n] if t < 2 else a["x_sample"].rearrange("b s d -> (b s) d")
                    sp.dma_start(xrow[0:n, t, :], src).then_inc(A[f"x{t}"], 16)
                for i, (name, r0, r1) in enumerate((("norm_attn_g", 0, 16), ("norm_ffn_g", 16, 32),
                                                    ("g_sb_out", 32, 40), ("g_fox_out", 40, 48))):
                    sp.dma_start(grow[r0:r1, :], a[name][0].rearrange("(c p) -> c p", p=P)).then_inc(A["g_in"], 16)
                for n in range(8):
                    if n >= 4:
                        sp.wait_ge(A["q_done"], 2 * (n - 4) + 2)
                    c0 = (n // 4) * 3 * H * HD + (n % 4) * 256
                    sp.dma_start(wq[:, n % 4, :, :], w_in[:, :, c0:c0 + 256]).then_inc(A[f"w{n % 4}"], 16)
                sp.wait_ge(A["tpose"], KC)
                sp.wait_ge(A["pt_in"], 16)
                for g in range(PAGES // 4 + 1):
                    load_keys(sp, S, kring, key_caches, ptr, g, n_phys)
                sp.wait_ge(A["lf"], 1)
                sp.dma_start(logf_p[0, 0].rearrange("(t p) h -> p t h", p=P), lf[:, 0:2, :]).then_inc(A["lst"], 16)
                sp.dma_start(logf_s[0].rearrange("b s h -> (b s) h"), lf[0:NB, 2, :]).then_inc(A["lst"], 16)
                sp.wait_ge(A["lst"], 32)

            @block.gpsimd
            def _(pool):
                own = Steps(pool, A["pool"])
                own.step(pool.memset(ones[:, :], 1.0))
                own.step(pool.memset(neg_sb[:, :], 0.0))

                def select(out, src, op, base, pattern, mult, fill):
                    own.step(pool.affine_select(out=out, in_=src, compare_op=op, fill=fill, base=base,
                                                pattern=pattern, channel_multiplier=mult))
                select(ident[:, :], ones[:, :], ALU.is_equal, 0, [[-1, P]], 1, 0.0)
                select(tri_ge[:, :], ones[:, :], ALU.is_ge, 0, [[-1, P]], 1, 0.0)
                select(tri_gt[:, :], ones[:, :], ALU.is_ge, -1, [[-1, P]], 1, 0.0)
                select(tri_le[:, :], ones[:, :], ALU.is_ge, 0, [[1, P]], -1, 0.0)
                select(tri_lt[:, :], ones[:, :], ALU.is_ge, -1, [[1, P]], -1, 0.0)
                select(neg_fx[:, :], neg_sb[:, :], ALU.is_ge, 0, [[-1, P]], 1, NEG)
                select(neg_sb[:, :], neg_sb[:, :], ALU.is_ge, -1, [[1, P]], -1, NEG)
                lv = later[:, :].rearrange("p (b j) -> p b j", j=PAGES)
                ov = ones[:, :].rearrange("p (b j) -> p b j", j=PAGES)
                select(lv, ov, ALU.is_ge, -1, [[PAGES, NB], [1, PAGES]], -1, 0.0)
                select(lv, lv, ALU.is_ge, 0, [[-PAGES, NB], [0, PAGES]], 1, 0.0)
                select(pick4[:, :, :], ones[:, 0:32].rearrange("p (a h) -> p a h", h=H), ALU.is_equal, 0,
                       [[-32, 4], [-1, H]], 1, 0.0)
                select(lastq4[:, :, :], ones[:, 0:32].rearrange("p (a h) -> p a h", h=NB), ALU.is_equal, -24,
                       [[-32, 4], [-1, NB]], 1, 0.0)
                own.step(pool.memset(lastq[:, :], 0.0))
                own.step(pool.memset(seg[:, :, :], 1.0))
                own.step(pool.memset(seg[:, :, 0:1], 0.0))
                own.step(pool.memset(fl[:, :], 0.0))
                own.step(pool.memset(lf[:, :, :], 0.0))
                own.step(pool.memset(wr[:, :, NG + NE:64], 0.0))
                pool.memset(ltot[:, :], 0.0).then_inc(s_const, 1)
                pool.wait_ge(A["ptc_in"], 16)
                pool.indirect_dma_start(
                    lfr[:, :], None, a["cache_fox_logf"][0].rearrange("n p h -> n (p h)"),
                    bass.IndirectOffsetOnAxis(ap=ptc[:, 0:1], axis=0)).then_inc(A["lfg"], 16)
                pool.wait_ge(A["tot"], 1)
                pool.tensor_copy(sel[:, :], lastq[:, 0:1].to_broadcast([P, P])).then_inc(S["sel"], 1)

            @block.scalar
            def _(act):
                own = Steps(act, A["act"])
                act.dma_start(ptc[:, :], a["pages"].rearrange("a (n o) -> (a n) o", o=1)).then_inc(A["ptc_in"], 16)
                act.dma_start(ptr[:, :], a["pages"]).then_inc(A["pt_in"], 16)
                act.dma_start(wf[:, :, :], w_in[:, :, 6 * H * HD + H - 32:6 * H * HD + H]).then_inc(A["wf_in"], 16)
                act.dma_start(bf[:, :], a["b_forget"].to_broadcast([P, H])).then_inc(A["bf_in"], 16)
                act.dma_start(wr[:, :, 0:NG], a["w_router_group"][0].rearrange("(c p) g -> p c g", p=P)).then_inc(A["wr_in"], 16)
                for g in range(NG):
                    act.dma_start(wr[:, :, NG + g * EPG:NG + (g + 1) * EPG],
                                  a["w_router_expert"][0, g].rearrange("(c p) e -> p c e", p=P)).then_inc(A["wr_in"], 16)
                act.dma_start(br[:, 0:NG], a["b_router_group"].to_broadcast([P, NG])).then_inc(A["wr_in"], 16)
                act.dma_start(br[:, NG:NG + NE],
                              a["b_router_expert"].rearrange("l g e -> l (g e)").to_broadcast([P, NE])).then_inc(A["wr_in"], 16)
                for i in range(4):
                    act.wait_ge(A["tcopy"], 4 * i + 4)
                    nc.scalar.activation(qo[:, 4 * i:4 * i + 4, :].rearrange("p c t -> p (c t)"),
                                         xT[:, 4 * i:4 * i + 4, :].rearrange("p c t -> p (c t)"), ACT.Square).then_inc(A["sq"], 1)
                act.wait_ge(A["ms"], 1)
                nc.scalar.activation(rst[:, :], rst[:, :], ACT.Sqrt).then_inc(A["sqrt"], 1)

                def heads(n):
                    for m in range(2):
                        h = 2 * n + m
                        act.wait_ge(A["q_done"], h + 1)
                        nc.scalar.activation(qo[:, h, :], bank[4 + h % 4][:, 0:T], ACT.Copy).then_inc(A["q_evac"], 1)

                def partial(i):
                    act.wait_ge(A["qp"], 2 * i + 2)
                    nc.scalar.activation(qpart[:, i * 512:(i + 1) * 512], bank[i][:, :], ACT.Copy).then_inc(A["qpc"], 1)

                heads(0)
                partial(0)
                heads(1)
                heads(2)
                partial(1)
                heads(3)
                act.wait_ge(A["fl"], 2)
                own.step(nc.scalar.activation(fa[:, :], fl[:, :], ACT.Abs))
                own.step(nc.scalar.activation(fa[:, :], fa[:, :], ACT.Exp, scale=-1.0))
                nc.scalar.activation(fa[:, :], fa[:, :], ACT.Ln, bias=1.0).then_inc(A["fln"], 1)
                heads(4)
                partial(2)
                partial(3)
                copy_queries(nc, act, S, bank[0:4], qb, 0)
                for n in range(5, 8):
                    heads(n)
                act.wait_ge(A["wr_in"], 16 * 7)
                act.wait_ge(A["pt_in"], 16)

            @block.tensor
            def _(pe):
                pe.wait_ge(s_const, 1)
                for t in range(3):
                    pe.wait_ge(A[f"x{t}"], 16)
                for c in range(KC):
                    if c >= 4:
                        pe.wait_ge(A["tcopy"], c - 3)
                    for t, (lo, n) in enumerate(TILES):
                        mm = pe.transpose(bank[c % 4][:, lo:lo + n], xrow[0:n, t, c * P:(c + 1) * P], ident[0:n, 0:n])
                    mm.then_inc(A["tpose"], 1)
                pe.wait_ge(A["g_in"], 64)
                pe.transpose(bank[4][:, 0:48], grow[:, :], ident[0:48, 0:48]).then_inc(A["gt"], 1)
                for c in range(KC):
                    if c % 4 == 0:
                        pe.wait_ge(A["sq"], c // 4 + 1)
                    mm = pe.matmul(bank[5][:, 0:T], ones[:, :], qo[:, c, :], start=(c == 0), stop=(c == KC - 1))
                mm.then_inc(A["ss"], 1)

                def partial(n):
                    pe.wait_ge(A[f"w{n % 4}"], 16 * (n // 4) + 16)
                    for c in range(KC):
                        u = c % 4
                        mm = pe.matmul(bank[n // 2][32 * u:32 * u + 32, n % 2 * 256:n % 2 * 256 + 256], xn[:, c, T - 32:T],
                                       wq[:, n % 4, c, :], start=(c < 4), stop=(c >= KC - 4))
                    mm.then_inc(A["qp"], 1)

                def heads(n):
                    if n >= 2:
                        pe.wait_ge(A["q_evac"], 2 * n - 2)
                    for m in range(2):
                        for c in range(KC):
                            mm = pe.matmul(bank[4 + (2 * n + m) % 4][:, 0:T], wq[:, n % 4, c, m * P:(m + 1) * P], xn[:, c, :],
                                           start=(c == 0), stop=(c == KC - 1))
                        mm.then_inc(A["q_done"], 1)

                pe.wait_ge(A["xn"], KC)
                for n in range(4):
                    partial(n)
                    heads(n)
                pe.wait_ge(A["wf_in"], 16)
                pe.wait_ge(A["qpc"], 2)
                for c in range(KC):
                    u = c % 4
                    mm = pe.matmul(bank[0][32 * u:32 * u + 32, 0:T], wf[:, c, :], xn[:, c, :],
                                   start=(c < 4), stop=(c >= KC - 4))
                mm.then_inc(A["fp"], 1)
                pe.wait_ge(A["lfg"], 16)
                lv = lfr[:, :].rearrange("n (p h) -> n h p", h=H)
                for h in range(H):
                    mm = pe.transpose(bank[2 + h // 4][:, (h % 4) * P:(h % 4 + 1) * P], lv[:, h, :], ident[:, :])
                mm.then_inc(A["lft"], 1)
                pe.wait_ge(A["fpc"], 1)
                for t, (lo, n) in enumerate(TILES):
                    mm = pe.matmul(bank[1][0:n, t * H:(t + 1) * H], fpart[:, lo:lo + n], lastq[:, 0:H], start=True, stop=True)
                mm.then_inc(A["f"], 1)
                pe.wait_ge(A["ltc"], 2)
                pe.wait_ge(A["tot"], 1)
                for half in range(2):
                    out = bank[2 + half]
                    pe.matmul(out[:, :], tri_gt[:, :], LFT[:, half * 512:(half + 1) * 512], start=True, stop=False,
                              skip_group_check=True)
                    for k in range(4):
                        mm = pe.matmul(out[:, k * P:(k + 1) * P], totb[:, half * 4 + k, :], later[:, :],
                                       start=False, stop=(k == 3), skip_group_check=True)
                mm.then_inc(A["fb"], 1)
                pe.wait_ge(A["w0"], 32)
                heads(4)
                pe.wait_ge(A["fbc"], 2)
                for n in range(4, 8):
                    partial(n)
                pe.wait_ge(A["lf"], 1)
                pe.matmul(bank[1][0:H, 0:P], lf[:, 0, :], tri_le[:, :], start=True, stop=True)
                pe.matmul(bank[1][0:H, P:SEQ], lf[:, 0, :], ones[:, :], start=True, stop=False)
                pe.matmul(bank[1][0:H, P:SEQ], lf[:, 1, :], tri_le[:, :], start=False, stop=True).then_inc(A["ct"], 1)
                pe.wait_ge(A["qpc"], 4)
                pe.wait_ge(A["ctc"], 1)
                broadcast_queries(pe, S, bank[0:4], sel, qpart, 0)
                for n in range(5, 8):
                    heads(n)

            @block.vector
            def _(dve):
                own = Steps(dve, A["dve"])
                for c in range(KC):
                    dve.wait_ge(A["tpose"], c + 1)
                    dve.tensor_copy(xT[:, c, :], bank[c % 4][:, 0:T]).then_inc(A["tcopy"], 1)
                dve.wait_ge(s_const, 1)
                own.step(dve.tensor_reduce(pick[:, :], pick4[:, :, :].rearrange("p a h -> p h a"), AX, ALU.add))
                own.step(dve.tensor_reduce(lastq[:, 0:NB], lastq4[:, :, :].rearrange("p a h -> p h a"), AX, ALU.add))
                dve.wait_ge(A["gt"], 1)
                own.step(dve.tensor_copy(gcol[:, :], bank[4][:, 0:48]))
                dve.wait_ge(A["ss"], 1)
                dve.tensor_scalar(rst[:, :], bank[5][:, 0:T], 1.0 / D, EPS, ALU.mult, ALU.add).then_inc(A["ms"], 1)
                dve.wait_ge(A["sqrt"], 1)
                own.step(dve.reciprocal(rstd[:, :], rst[:, :]))
                for c in range(KC):
                    dve.scalar_tensor_tensor(out=xn[:, c, :], in0=xT[:, c, :], scalar=gcol[:, G_ATTN + c:G_ATTN + c + 1],
                                             in1=rstd[:, :], op0=ALU.mult, op1=ALU.mult).then_inc(A["xn"], 1)
                dve.wait_ge(A["lfg"], 16)
                own.step(dve.tensor_reduce(ltot[:, :], lfr[:, :].rearrange("n (p h) -> n h p", h=H), AX, ALU.add))
                dve.tensor_copy(totb[:, :, :], over(ltot[:, :], P)).then_inc(A["tot"], 1)
                dve.wait_ge(A["fp"], 1)
                dve.tensor_copy(fpart[:, :], bank[0][:, 0:T]).then_inc(A["fpc"], 1)
                dve.wait_ge(A["lft"], 1)
                for i in range(2):
                    dve.tensor_copy(LFT[:, i * 512:(i + 1) * 512], bank[2 + i][:, :]).then_inc(A["ltc"], 1)
                dve.wait_ge(A["f"], 1)
                dve.wait_ge(A["bf_in"], 16)
                bfv = bf[:, :].rearrange("p (t h) -> p t h", t=1)
                dve.tensor_tensor(fl[:, 0:2 * H].rearrange("p (t h) -> p t h", h=H),
                                  bank[1][:, 0:2 * H].rearrange("p (t h) -> p t h", h=H),
                                  bfv.to_broadcast([P, 2, H]), ALU.add).then_inc(A["fl"], 1)
                dve.tensor_tensor(fl[0:NB, 2 * H:3 * H], bank[1][0:NB, 2 * H:3 * H], bf[0:NB, :], ALU.add).then_inc(A["fl"], 1)
                dve.wait_ge(A["fl"], 2)
                own.step(dve.tensor_scalar(fr[:, :], fl[:, :], -1.0, 0.0, ALU.mult, ALU.max))
                dve.wait_ge(A["fb"], 1)
                for i in range(2):
                    dve.tensor_copy(
                        FB[:, :, i * 64:(i + 1) * 64].rearrange("p b (h j) -> p h b j", j=PAGES),
                        bank[2 + i][:, :].rearrange("p (h b j) -> p h b j", h=4, j=PAGES)).then_inc(A["fbc"], 1)
                dve.wait_ge(A["fln"], 1)
                dve.scalar_tensor_tensor(out=lf[:, :, :].rearrange("p t h -> p (t h)"), in0=fr[:, :], scalar=-1.0,
                                         in1=fa[:, :], op0=ALU.mult, op1=ALU.subtract).then_inc(A["lf"], 1)
                dve.wait_ge(A["ct"], 1)
                dve.tensor_scalar(cTs[:, :], bank[1][0:H, 0:SEQ], -1.0 / SCALE, None, ALU.mult).then_inc(A["ctc"], 1)
                for q in range(4):
                    score(dve, S, kring, qb, Z, 0, q)
                dve.wait_ge(A["fbc"], 2)
        actx.close()
        done_with(nc, A)

        attention(nc, a, ident, ones, tri_ge, tri_lt, neg_sb, neg_fx, pick, lastq, seg, xn, qo, lf, qpart, cTs, FB,
                  ptr, ws, W, kring, qb, sel, Z, key_caches, w_in, bank, S, outs)
        bctx.close()
        ffn(nc, ctx, ws, W, a, ident, ones, tri_lt, gcol, xT, xn, qo, wr, br, bank, sem, y_prompt, y_sample,
            u_rows, y_rows)


DVE_TURN = 22
ACT_TURN = 4


def attention(nc, a, ident, ones, tri_ge, tri_lt, neg_sb, neg_fx, pick, lastq, seg, xn, qo, lf, qpart, cTs, FB,
              ptr, ws, W, kring, qb, sel, Z, key_caches, w_in, bank, S, outs):
    (_, _, sbk_p, sbv_p, fxk_p, fxv_p, _, sbk_s, sbv_s, fxk_s, fxv_s, _) = outs
    ctx = ExitStack()
    with ctx:
        def sb(name, shape, dt=F32):
            return ctx.enter_context(nc.sbuf_tensor(name, shape, dt))

        vring = ws[:, 2:4, :].rearrange("p s (a g f) -> p (s a) g f", a=2, g=2)
        wkv = ws[:, 4, :].rearrange("p (i c d) -> p i c d", i=2, c=KC)
        osum = ws[:, 5, 0:4 * 512].rearrange("p (i d) -> p i d", i=4)
        kT = [sb(f"kT{g}", [P, T]) for g in range(2)]
        vT = [sb(f"vT{g}", [P, T]) for g in range(2)]
        krow = [sb(f"krow{g}", [P, 3, HD]) for g in range(2)]
        vrow = [sb(f"vrow{g}", [P, 3, HD]) for g in range(2)]
        qf = sb("qf", [P, SEQ])
        cm = sb("cm", [H, SEQ])
        ecol = sb("ecol", [H, 1])
        stay = sb("stay", [P, 384])
        pos_z = sb("pos_z", [P, 384])
        att = sb("att", [P, 384])
        zf = sb("zf", [P, 384])
        pf = sb("pf", [P, 384])
        pT = sb("pT", [P, 384])
        nmax = sb("nmax", [P, 2])
        rsum = sb("rsum", [P, 2])
        rinv = sb("rinv", [P, 2])
        zs = sb("zs", [P, H * PAGES])
        zr = sb("zr", [P, H * PAGES])
        sp_h = sb("sp_h", [P, H, PAGES + 1])
        run = sb("run", [P, H, PAGES + 1])
        ts = sb("ts", [P, H * PAGES])
        zx = sb("zx", [P, H * PAGES])
        mxp = sb("mxp", [P, H])
        m8 = sb("m8", [H, 1])
        diag = sb("diag", [H, H])
        dsum = sb("dsum", [P, H])
        PR = ws[:, 5, 4 * 512:4 * 512 + 2 * PAGES * 32].rearrange("p (g j h) -> p g j h", g=2, j=PAGES)
        MX = sb("MX", [P, NB, H])
        DEN = sb("DEN", [P, NB, H])
        OF = sb("OF", [P, NB, H])
        QK = sb("QK", [P, H, NB])
        VN = sb("VN", [P, H, NB])
        fin = [sb(f"fin{i}", [P, H * NB]) for i in range(6)]
        ab = sb("ab", [P, 2, H * NB])
        dlf = sb("dlf", [NB, H, NB])

        value_caches = [a[n][0].rearrange("n p h d -> n p (h d)") for n in ("cache_sb_v", "cache_fox_v")]
        n_phys = a["cache_sb_k"].shape[1]
        GR = PAGES // 4

        bstack = ExitStack()
        block = bstack.enter_context(nc.Block())

        @block.sync
        def _(sp):
            def values(g, first=False):
                for u in range(4):
                    if not first:
                        sp.wait_ge(S["vused"], 4 * (g - 1) + u + 1)
                    page = sp.value_load(ptr[0:1, bass.ds(4 * g + u, 1)], min_val=0, max_val=n_phys - 1)
                    for k in range(2):
                        sp.dma_start(vring[:, u, k, :],
                                     value_caches[k][bass.ds(page, 1)].rearrange("a p f -> (a p) f")).then_inc(S[f"v{u}"], 16)

            values(0, first=True)
            with sp.Fori(GR + 1, NB * GR) as g:
                load_keys(sp, S, kring, key_caches, ptr, g, n_phys)
                values(g - GR)
            values((NB - 1) * GR)
            sp.wait_ge(S["kused"], NB * PAGES)
            for j in range(2):
                load_out(sp, a, ws, W, j)
            with sp.Fori((NB - 1) * GR + 1, NB * GR) as g:
                values(g)
            sp.wait_ge(S["proj3"], NB)
            load_expert(sp, a, ws, W, 0, 0)
            sp.wait_ge(S["vused"], NB * PAGES)
            for j in range(2, 4):
                load_out(sp, a, ws, W, j)

        @block.gpsimd
        def _(pool):
            own = Steps(pool, S["pool"])
            own.step(pool.memset(PR[:, :, :, :], 0.0))
            pool.memset(sp_h[:, :, :], 0.0).then_inc(S["pad"], 1)

            def select_sample(n):
                pool.wait_ge(S["bcast"], n)
                pool.tensor_copy(sel[:, :], lastq[:, bass.ds(n, 1)].to_broadcast([P, P])).then_inc(S["sel"], 1)

            select_sample(1)

            def turn(b, last):
                wait_past(pool, S["cm"], b)
                wait_past(pool, S["fxz"], b)
                pool.tensor_copy(qf[:, :], at(qo, b + H, 0, SEQ)).then_inc(S["qf"], 1)
                own.step(pool.tensor_copy(ecol[:, :], ident[0:H, bass.ds(b, 1)]))
                pool.tensor_tensor(cm[:, :], cTs[:, :], ecol[:, 0:1].to_broadcast([H, SEQ]), ALU.mult).then_inc(S["cm"], 1)
                if not last:
                    select_sample(b + 2)

            turn(0, False)
            with pool.Fori(1, NB - 1) as b:
                own.enter(b, 1, 1)
                turn(b, False)
            own.leave(NB - 2)
            turn(NB - 1, True)

        @block.tensor
        def _(pe):
            def project(i, b):
                pe.wait_ge(S[f"w{i % 2}"], 32 * b + 16 * (i // 2) + 16)
                out = bank[4 + i % 2]
                for c in range(KC):
                    mm = pe.matmul(out[:, 0:T], wkv[:, i % 2, c, :], xn[:, c, :], start=(c == 0), stop=(c == KC - 1))
                mm.then_inc(S[f"proj{i}"], 1)

            def rows(i, src, out, b):
                pe.wait_ge(S[f"kv{i}"], b + 1)
                for t, (lo, n) in enumerate(TILES):
                    mm = pe.transpose(out[0:n, t * P:(t + 1) * P], src[:, lo:lo + n], ident[:, :])
                mm.then_inc(S[f"tr{i}"], 1)

            def values(b, q):
                for u in range(4):
                    t = 4 * q + u
                    pe.wait_ge(S[f"v{u}"], 32 * (4 * b + q + 1))
                    for g in range(2):
                        for half in range(2):
                            mm = pe.matmul(bank[2 * g + half][32 * u:32 * u + 32, :], PR[:, g, t, :],
                                           vring[:, u, g, half * 512:(half + 1) * 512],
                                           start=(t < 4), stop=(t >= PAGES - 4))
                    mm.then_inc(S["vused"], 1)

            def weights(n, extract):
                pe.wait_ge(S["mx"], n + 1)
                pe.transpose(bank[4][0:H, 0:P], mxp[:, :], ident[:, :]).then_inc(S["mxT"], 1)
                pe.wait_ge(S["ssp"], n + 1)
                pe.matmul(bank[5][:, 0:P], tri_ge[:, :], sp_h[:, :, 1:PAGES + 1], start=True, stop=False)
                pe.matmul(bank[5][:, 0:P], ones[:, :], run[:, :, 0:PAGES], start=False, stop=True).then_inc(S["C2"], 1)
                pe.wait_ge(S["diag"], n + 1)
                pe.matmul(bank[4][:, P:P + H], ones[0:H, :], diag[:, :], start=True, stop=True).then_inc(S["mb"], 1)
                if extract:
                    outputs(n - 1)
                pe.wait_ge(S["dsum"], n + 1)
                pe.wait_ge(S["ts"], n + 1)
                pe.matmul(bank[5][:, 256:256 + H], ones[:, :], dsum[:, :], start=True, stop=True).then_inc(S["den"], 1)
                pe.wait_ge(S["zx"], n + 1)
                pe.wait_ge(S["denc"], n + 1)

            def outputs(b):
                pe.wait_ge(S["osum"], 4 * b + 4)
                pe.wait_ge(S["sboc"], b + 1)
                for i in range(2 * H):
                    mm = pe.matmul(bank[6][:, i:i + 1], osum[:, i // 4, (i % 4) * P:(i % 4 + 1) * P],
                                   pick[:, i % H:i % H + 1], start=True, stop=True)
                mm.then_inc(S["ext"], 1)

            def prompt_out(row, w, out, done):
                pe.matmul(out[:, 0:SEQ], row[:, 0, :], w[:, 0:SEQ], start=True, stop=False)
                pe.matmul(out[:, P:SEQ], row[:, 1, :], w[:, SEQ:384], start=False, stop=True).then_inc(S[done], 1)

            def turn(b, last):
                pe.wait_ge(S["w_sb"], b + 1)
                pe.wait_ge(S["w_fx"], b + 1)
                values(b, 0)
                pe.wait_ge(S["qb"], 4 * (b + 2))
                project(0, b)
                project(1, b)
                rows(0, kT[0], bank[6], b)
                rows(1, vT[0], bank[7], b)
                project(2, b)
                project(3, b)
                values(b, 1)
                pe.wait_ge(S["row0"], b + 1)
                pe.matmul(bank[6][:, 0:SEQ], kT[0][:, 0:P], at(qo, b, 0, SEQ), start=True, stop=True)
                pe.matmul(bank[6][:, SEQ:384], kT[0][:, P:SEQ], at(qo, b, P, SEQ), start=True, stop=True).then_inc(S["sbz"], 1)
                pe.wait_ge(S["row1"], b + 1)
                rows(2, kT[1], bank[7], b)
                rows(3, vT[1], bank[4], b)
                pe.wait_ge(S["kv3"], b + 1)
                pe.wait_ge(S["qf"], b + 1)
                pe.wait_ge(S["cm"], b + 1)
                pe.matmul(bank[5][:, 0:P], qf[:, 0:P], kT[1][:, 0:P], start=True, stop=False)
                pe.matmul(bank[5][:, 0:P], ones[0:H, :], cm[:, 0:P], start=False, stop=True)
                pe.matmul(bank[5][:, P:384], qf[:, P:SEQ], kT[1][:, 0:SEQ], start=True, stop=False)
                pe.matmul(bank[5][:, P:384], ones[0:H, :], cm[:, :], start=False, stop=True).then_inc(S["fxz"], 1)
                pe.wait_ge(S["row2"], b + 1)
                pe.wait_ge(S["sp"], b + 1)
                pe.matmul(bank[7][:, 0:384], tri_ge[:, :], stay[:, :], start=True, stop=False, skip_group_check=True)
                pe.matmul(bank[7][:, P:SEQ], ones[:, :], stay[:, SEQ:384], start=False, stop=True,
                          skip_group_check=True).then_inc(S["C"], 1)
                values(b, 2)
                pe.wait_ge(S["at"], b + 1)
                prompt_out(vrow[0], att, bank[6], "sbo")
                pe.wait_ge(S["row3"], b + 1)
                pe.wait_ge(S["pn"], b + 1)
                for k in range(3):
                    mm = pe.transpose(bank[4][:, k * P:(k + 1) * P], pf[:, k * P:(k + 1) * P], ident[:, :])
                mm.then_inc(S["tp"], 1)
                pe.wait_ge(S["pT"], b + 1)
                if not last:
                    pe.wait_ge(S["sboc"], b + 1)
                    broadcast_queries(pe, S, bank[4:8], sel, qpart, b + 2)
                values(b, 3)
                if not last:
                    pe.wait_ge(S["qb"], 4 * b + 12)
                prompt_out(vrow[1], pT, bank[7], "fxo")
                if last:
                    outputs(b)
                else:
                    weights(b + 1, True)
                    pe.wait_ge(S["extc"], b + 1)
                    pe.wait_ge(S["fxoc"], b + 1)

            weights(0, False)
            broadcast_queries(pe, S, bank[4:8], sel, qpart, 1)
            turn(0, False)
            with pe.Fori(1, NB - 1) as b:
                turn(b, False)
            turn(NB - 1, True)
            pe.wait_ge(S["own_kv"], 2 * NB)
            pe.matmul(bank[4][:, 0:64], ones[:, :], QK[:, :, :], start=True, stop=True)
            pe.wait_ge(S["lfd"], 1)
            pe.matmul(bank[4][:, 64:128], ones[0:NB, :], dlf[:, :, :], start=True, stop=True).then_inc(S["done1"], 1)

        @block.scalar
        def _(act):
            own = Steps(act, S["act"])

            def load_w(i, b):
                c0 = (1 + i % 2 + 3 * (i // 2)) * H * HD
                src = w_in[:, :, c0:c0 + H * HD].rearrange("p c (h d) -> h p c d", d=HD)
                act.dma_start(wkv[:, i % 2, :, :], src[bass.ds(b, 1)].rearrange("a p c d -> (a p) c d")).then_inc(S[f"w{i % 2}"], 16)

            def copy(out, src, done):
                nc.scalar.activation(out, src, ACT.Copy).then_inc(S[done], 1)

            def softplus_1(out, z):
                own.step(nc.scalar.activation(out, z, ACT.Abs, scale=SCALE))
                own.step(nc.scalar.activation(out, out, ACT.Exp, scale=-1.0))
                return nc.scalar.activation(out, out, ACT.Ln, bias=1.0)

            def store(i, row, out_p, out_s, b):
                act.wait_ge(S[f"row{i}"], b + 1)
                act.dma_start(out_p[0, 0].rearrange("(t p) h d -> h p t d", p=P)[bass.ds(b, 1)].rearrange("a p t d -> (a p) t d"),
                               row[:, 0:2, :]).then_inc(S[f"st{i}"], 16)
                act.dma_start(out_s[0].rearrange("b s h d -> h (b s) d")[bass.ds(b, 1)].rearrange("a b d -> (a b) d"),
                               row[0:NB, 2, :]).then_inc(S[f"st{i}"], 16)

            def sample_softplus(n):
                act.wait_ge(S["kused"], PAGES * (n + 1))
                softplus_1(zs[:, :], Z[:, 0, :, :].rearrange("p h j -> p (h j)")).then_inc(S["ssl"], 1)

            def sample_weights(n):
                for g, src, ready, done in ((1, zx, "zx", "w_fx"), (0, ts, "ts", "w_sb")):
                    act.wait_ge(S[ready], n + 1)
                    nc.scalar.activation(PR[:, g, :, 0:H].rearrange("p j h -> p h j"),
                                         src[:, :].rearrange("p (h j) -> p h j", j=PAGES), ACT.Exp).then_inc(S[done], 1)

            def turn(b, last):
                act.wait_ge(S["proj0"], b + 1)
                copy(kT[0][:, :], bank[4][:, 0:T], "kv0")
                load_w(2, b)
                act.wait_ge(S["proj1"], b + 1)
                copy(vT[0][:, :], bank[5][:, 0:T], "kv1")
                load_w(3, b)
                act.wait_ge(S["proj2"], b + 1)
                wait_past(act, S["own_kv"], 2 * b)
                copy(kT[1][:, :], bank[4][:, 0:T], "kv2")
                if not last:
                    load_w(0, b + 1)
                act.wait_ge(S["proj3"], b + 1)
                copy(vT[1][:, :], bank[5][:, 0:T], "kv3")
                if not last:
                    load_w(1, b + 1)
                act.wait_ge(S["sbz"], b + 1)
                softplus_1(stay[:, :], bank[6][:, 0:384]).then_inc(S["sln"], 1)
                act.wait_ge(S["t"], b + 1)
                nc.scalar.activation(att[:, :], att[:, :], ACT.Exp).then_inc(S["at"], 1)
                store(0, krow[0], sbk_p, sbk_s, b)
                store(1, vrow[0], sbv_p, sbv_s, b)
                store(2, krow[1], fxk_p, fxk_s, b)
                store(3, vrow[1], fxv_p, fxv_s, b)
                act.wait_ge(S["zf"], b + 1)
                nc.scalar.activation(pf[:, 0:P], zf[:, 0:P], ACT.Exp, bias=nmax[:, 0:1], accum_out=rsum[:, 0:1]).then_inc(S["fp"], 1)
                nc.scalar.activation(pf[:, P:384], zf[:, P:384], ACT.Exp, bias=nmax[:, 1:2], accum_out=rsum[:, 1:2]).then_inc(S["fp"], 1)
                act.wait_ge(S["sbo"], b + 1)
                copy(at(qo, b, 0, SEQ), bank[6][:, 0:SEQ], "sboc")
                act.wait_ge(S["tp"], b + 1)
                copy(pT[:, :], bank[4][:, 0:384], "pT")
                if not last:
                    act.wait_ge(S["kused"], PAGES * (b + 2))
                    copy_queries(nc, act, S, bank[4:8], qb, b + 2)
                act.wait_ge(S["fxo"], b + 1)
                act.wait_ge(S["qf"], b + 1)
                copy(at(qo, b + H, 0, SEQ), bank[7][:, 0:SEQ], "fxoc")
                if not last:
                    sample_softplus(b + 1)
                act.wait_ge(S["vused"], PAGES * (b + 1))
                wait_past(act, S["ext"], b)
                for i in range(4):
                    copy(osum[:, i, :], bank[i][:, :], "osum")
                if not last:
                    sample_weights(b + 1)

            load_w(0, 0)
            load_w(1, 0)
            sample_softplus(0)
            act.wait_ge(S["pad"], 1)
            sample_weights(0)
            act.wait_ge(S["kused"], PAGES)
            copy_queries(nc, act, S, bank[4:8], qb, 1)
            turn(0, False)
            with act.Fori(1, NB - 1) as b:
                own.enter(b, 1, ACT_TURN)
                turn(b, False)
            own.leave(NB - 2)
            turn(NB - 1, True)
            for i in range(4):
                act.wait_ge(S[f"st{i}"], 32 * NB)
            act.wait_ge(S["done2"], 1)
            nc.scalar.activation(ab[:, :, :], ab[:, :, :], ACT.Exp).then_inc(S["done3"], 1)

        @block.vector
        def _(dve):
            own = Steps(dve, S["dve"])

            def by_head(x):
                return x.rearrange("p (h j) -> p h j", j=PAGES)

            z_sb = Z[:, 0, :, :].rearrange("p h j -> p (h j)")
            z_fx = Z[:, 1, :, :].rearrange("p h j -> p (h j)")

            def weights(n, extract):
                dve.wait_ge(S["kused"], PAGES * (n + 1))
                own.step(dve.scalar_tensor_tensor(out=zx[:, :], in0=z_fx, scalar=SCALE,
                                                  in1=FB[:, bass.ds(n, 1), :].rearrange("p a f -> p (a f)"),
                                                  op0=ALU.mult, op1=ALU.add))
                dve.tensor_reduce(mxp[:, :], by_head(zx[:, :]), AX, ALU.max).then_inc(S["mx"], 1)
                own.step(dve.tensor_scalar(zr[:, :], z_sb, SCALE, 0.0, ALU.mult, ALU.max))
                dve.wait_ge(S["ssl"], n + 1)
                own.step(dve.tensor_tensor(sp_h[:, :, 1:PAGES + 1], by_head(zr[:, :]), by_head(zs[:, :]), ALU.add))
                flat = lambda x: x[:, :, :].rearrange("p h j -> p (h j)")
                dve.tensor_tensor_scan(flat(run), flat(seg), flat(sp_h), 0.0,
                                       ALU.mult, ALU.add).then_inc(S["ssp"], 1)
                dve.wait_ge(S["mxT"], n + 1)
                own.step(dve.tensor_reduce(m8[:, :], bank[4][0:H, 0:P], AX, ALU.max))
                dve.tensor_scalar(diag[:, :], ident[0:H, 0:H], m8[:, 0:1], None, ALU.mult).then_inc(S["diag"], 1)
                dve.wait_ge(S["C2"], n + 1)
                dve.scalar_tensor_tensor(out=ts[:, :], in0=z_sb, scalar=SCALE, in1=bank[5][:, 0:P],
                                         op0=ALU.mult, op1=ALU.subtract).then_inc(S["ts"], 1)
                dve.wait_ge(S["mb"], n + 1)
                mx = MX[:, bass.ds(n, 1), :].rearrange("p a h -> p (a h)")
                own.step(dve.tensor_copy(mx, bank[4][:, P:P + H]))
                dve.tensor_tensor(by_head(zx[:, :]), by_head(zx[:, :]), over(mx, PAGES), ALU.subtract).then_inc(S["zx"], 1)
                dve.wait_ge(S["w_fx"], n + 1)
                dve.tensor_reduce(dsum[:, :], PR[:, 1, :, 0:H].rearrange("p j h -> p h j"), AX, ALU.add).then_inc(S["dsum"], 1)
                if extract:
                    outputs(n - 1)
                dve.wait_ge(S["den"], n + 1)
                dve.tensor_copy(DEN[:, bass.ds(n, 1), :].rearrange("p a h -> p (a h)"), bank[5][:, 256:256 + H]).then_inc(S["denc"], 1)

            def outputs(b):
                dve.wait_ge(S["ext"], b + 1)
                own.step(dve.tensor_copy(qo[:, 0:H, bass.ds(SEQ + b, 1)].rearrange("p h a -> p (h a)"), bank[6][:, 0:H]))
                dve.tensor_copy(OF[:, bass.ds(b, 1), :].rearrange("p a h -> p (a h)"), bank[6][:, H:2 * H]).then_inc(S["extc"], 1)

            def row_copy(i, src, row, b):
                dve.wait_ge(S[f"tr{i}"], b + 1)
                wait_past(dve, S[f"st{i}"], 32 * b)
                own.step(dve.tensor_copy(row[:, 0:2, :], src[:, 0:SEQ].rearrange("p (t d) -> p t d", d=HD)))
                dve.tensor_copy(row[0:NB, 2, :], src[0:NB, SEQ:384]).then_inc(S[f"row{i}"], 1)

            def turn(b, last):
                def diag_op(buf, mask, op):
                    for lo in (0, SEQ):
                        ins = dve.tensor_tensor(buf[:, lo:lo + P], buf[:, lo:lo + P], mask[:, :], op)
                        if lo == 0:
                            own.step(ins)
                    return ins

                if not last:
                    score(dve, S, kring, qb, Z, b + 1, 0)
                row_copy(0, bank[6], krow[0], b)
                row_copy(1, bank[7], vrow[0], b)
                if not last:
                    score(dve, S, kring, qb, Z, b + 1, 1)
                dve.wait_ge(S["sln"], b + 1)
                own.step(dve.tensor_scalar(pos_z[:, :], bank[6][:, 0:384], SCALE, 0.0, ALU.mult, ALU.max))
                own.step(dve.tensor_tensor(stay[:, :], stay[:, :], pos_z[:, :], ALU.add))
                diag_op(stay, tri_lt, ALU.mult).then_inc(S["sp"], 1)
                row_copy(2, bank[7], krow[1], b)
                row_copy(3, bank[4], vrow[1], b)
                dve.wait_ge(S["kv3"], b + 1)
                dve.tensor_tensor(QK[:, bass.ds(b, 1), :].rearrange("p a n -> p (a n)"), at(qo, b + H, SEQ, T), kT[1][:, SEQ:T],
                                  ALU.mult).then_inc(S["own_kv"], 1)
                dve.tensor_copy(VN[:, bass.ds(b, 1), :].rearrange("p a n -> p (a n)"), vT[1][:, SEQ:T]).then_inc(S["own_kv"], 1)
                if not last:
                    score(dve, S, kring, qb, Z, b + 1, 2)
                dve.wait_ge(S["C"], b + 1)
                own.step(dve.tensor_copy(pos_z[:, :], bank[7][:, 0:384]))
                own.step(dve.scalar_tensor_tensor(out=att[:, :], in0=bank[6][:, 0:384], scalar=SCALE, in1=pos_z[:, :],
                                                  op0=ALU.mult, op1=ALU.subtract))
                diag_op(att, neg_sb, ALU.add).then_inc(S["t"], 1)
                dve.wait_ge(S["fxz"], b + 1)
                own.step(dve.tensor_scalar(zf[:, :], bank[5][:, 0:384], SCALE, None, ALU.mult))
                own.step(diag_op(zf, neg_fx, ALU.add))
                own.step(dve.tensor_reduce(nmax[:, 0:1], zf[:, 0:P], AX, ALU.max, negate=True))
                dve.tensor_reduce(nmax[:, 1:2], zf[:, P:384], AX, ALU.max, negate=True).then_inc(S["zf"], 1)
                dve.wait_ge(S["fp"], 2 * b + 2)
                own.step(dve.reciprocal(rinv[:, :], rsum[:, :]))
                own.step(dve.tensor_scalar(pf[:, 0:P], pf[:, 0:P], rinv[:, 0:1], None, ALU.mult))
                dve.tensor_scalar(pf[:, P:384], pf[:, P:384], rinv[:, 1:2], None, ALU.mult).then_inc(S["pn"], 1)
                if last:
                    outputs(b)
                else:
                    score(dve, S, kring, qb, Z, b + 1, 3)
                    weights(b + 1, True)

            dve.wait_ge(S["pad"], 1)
            weights(0, False)
            turn(0, False)
            with dve.Fori(1, NB - 1) as b:
                own.enter(b, 1, DVE_TURN)
                turn(b, False)
            own.leave(NB - 2)
            turn(NB - 1, True)
            idh = ident[0:NB, 0:NB].rearrange("b (h n) -> b h n", h=1).to_broadcast([NB, H, NB])
            dve.tensor_tensor(dlf[:, :, :], over(lf[0:NB, 2, :], NB), idh, ALU.mult).then_inc(S["lfd"], 1)
            dve.wait_ge(S["done1"], 1)

            def hb(x):
                return x[:, :].rearrange("p (h b) -> p h b", b=NB)

            mxv = MX[:, :, :].rearrange("p b h -> p h b")
            own_z, top, den, rec, num, num2 = fin
            dve.wait_ge(S["extc"], NB)
            dve.wait_ge(S["denc"], NB)
            own.step(dve.tensor_copy(top[:, :], bank[4][:, 64:128]))
            own.step(dve.scalar_tensor_tensor(out=own_z[:, :], in0=bank[4][:, 0:64], scalar=SCALE, in1=top[:, :],
                                              op0=ALU.mult, op1=ALU.subtract))
            own.step(dve.tensor_tensor(hb(top), mxv, hb(own_z), ALU.max))
            own.step(dve.tensor_tensor(ab[:, 0, :].rearrange("p (h b) -> p h b", b=NB), mxv, hb(top), ALU.subtract))
            dve.tensor_tensor(ab[:, 1, :], own_z[:, :], top[:, :], ALU.subtract).then_inc(S["done2"], 1)
            dve.wait_ge(S["done3"], 1)
            av = ab[:, 0, :].rearrange("p (h b) -> p h b", b=NB)
            own.step(dve.tensor_tensor(hb(den), DEN[:, :, :].rearrange("p b h -> p h b"), av, ALU.mult))
            own.step(dve.tensor_tensor(den[:, :], den[:, :], ab[:, 1, :], ALU.add))
            own.step(dve.reciprocal(rec[:, :], den[:, :]))
            own.step(dve.tensor_tensor(hb(num), OF[:, :, :].rearrange("p b h -> p h b"), av, ALU.mult))
            own.step(dve.tensor_tensor(num2[:, :], VN[:, :, :].rearrange("p h n -> p (h n)"), ab[:, 1, :], ALU.mult))
            own.step(dve.tensor_tensor(num[:, :], num[:, :], num2[:, :], ALU.add))
            own.step(dve.tensor_tensor(qo[:, H:2 * H, SEQ:T], hb(num), hb(rec), ALU.mult))
        bstack.close()
    done_with(nc, S)


G_FFN, G_GRP = 16, 32
ROUTE_BIG = 1.0e30
HALF = SLOTS // 2


def ffn(nc, ctx, ws, W, a, ident, ones, tri_lt, gcol, xT, xn, qo, wr, br, bank, sem, y_prompt, y_sample,
        u_rows, y_rows):
    def sb(name, shape, dt=F32, where=ctx):
        return where.enter_context(nc.sbuf_tensor(name, shape, dt))

    idx = sb("idx", [P, PAIRS], I32)
    dest = sb("dest", [P, BLOCKS], I32)
    gates = sb("gates", [P, 3, 2])
    extra = sb("extra", [1, 2, EXTRA], I32)
    many = sb("many", [1, BLOCKS], I32)
    many2 = sb("many2", [1, PAIRS], I32)

    xg = sb("xg", [P, D])
    cctx = ExitStack()
    rst = sb("c_rst", [P, 2, T], where=cctx)
    rstd = sb("c_rstd", [P, 2, T], where=cctx)
    stage = sb("stage", [P, 2, D], where=cctx)
    io32 = sb("io32", [P, P], I32, where=cctx)
    iota = sb("iota", [P, P], where=cctx)
    slot_of = sb("slot_of", [P, P], where=cctx)
    manyf = sb("manyf", [1, BLOCKS], where=cctx)
    tok = sb("tok", [P, 3], where=cctx)
    tokc = sb("tokc", [P, 3], where=cctx)
    toki = sb("toki", [P, 3], I32, where=cctx)
    valid = sb("valid", [P, 3], where=cctx)
    thr = sb("thr", [P, 4], where=cctx)
    lpart = sb("lpart", [P, T], where=cctx)
    fold = sb("fold", [P, NG + NE], where=cctx)
    lg = sb("lg", [P, 3, NG + NE], where=cctx)
    mask = sb("mask", [P, 3, NE], where=cctx)
    ext = sb("ext", [NE, P], where=cctx)
    ohs = sb("ohs", [P, 3, 2, P], where=cctx)
    ohb = sb("ohb", [P, 3, 2, PAIRS], where=cctx)
    r2 = sb("r2", [P, 3, 5], where=cctx)
    gmx = sb("gmx", [P, 3], where=cctx)
    rg = sb("rg", [P, 3, NG], where=cctx)
    re_ = sb("re_", [P, 3, NE], where=cctx)
    tmp = sb("r_tmp", [P, 3, NE], where=cctx)
    oh = [sb(f"oh{k}", [P, 3, NE], where=cctx) for k in range(2)]
    gsel = sb("gsel", [P, 3, NG], where=cctx)
    top = [sb(f"top{k}", [P, 3], where=cctx) for k in range(2)]
    eid = sb("eid", [P, 3, 2], where=cctx)
    rank = sb("rank", [P, 3, 2], where=cctx)
    full = sb("full", [P, 3, 2], where=cctx)
    first = sb("first", [P, 3, 2], where=cctx)
    pre = sb("pre", [P, 3, 2], where=cctx)
    in_blk = sb("in_blk", [P, 3, 2], where=cctx)
    odd = sb("odd", [P, 3, 2], where=cctx)
    blk = sb("blk", [P, 3, 2], where=cctx)
    cmp6 = sb("cmp6", [P, 3, 2, 4], where=cctx)
    ohs2 = sb("ohs2", [P, 3, 2, P], where=cctx)
    ohb2 = sb("ohb2", [P, 3, 2, BLOCKS], where=cctx)
    slot2_of = sb("slot2_of", [P, P], where=cctx)
    destc = sb("destc", [P, 3, 2], where=cctx)
    drow = sb("drow", [P, 1], where=cctx)
    dtmp = sb("dtmp", [P, 4], where=cctx)
    small = sb("small", [P, 3, 2], where=cctx)
    cnt4 = sb("cnt4", [NE, 4, P], where=cctx)
    base = sb("base", [P, 2, NE], where=cctx)
    xb = sb("xb", [1, EXTRA, NE], where=cctx)
    xb2 = sb("xb2", [1, EXTRA, NE], where=cctx)
    xo = sb("xo", [1, 2, EXTRA], where=cctx)
    rks = sb("rks", [P, 3, NE], where=cctx)
    C = {n: sem("c_" + n) for n in (
        "sq ss ms sqrt on o_done h sq2 ss2 ms2 sqrt2 un lp lpc lgp rt rcopy rst0 rst1 iota ex "
        "mask cnt pe2 oh idxp idx act dve pool gg").split()}

    def mean_square(dve, out, ps, n, ms):
        dve.tensor_scalar(rst[:, out, :], ps, 1.0 / n, EPS, ALU.mult, ALU.add).then_inc(C[ms], 1)

    with nc.Block() as block:
        @block.sync
        def _(sp):
            load_expert(sp, a, ws, W, 1, 0)
            for j in range(4, 8):
                sp.wait_ge(C["o_done"], 2 * (j - 4) + 2)
                load_out(sp, a, ws, W, j)
            for k in range(2, 6):
                sp.wait_ge(C["o_done"], 2 * (4 + SLOT[k]) + 2)
                load_expert(sp, a, ws, W, k, k // 3)

        @block.gpsimd
        def _(pool):
            own = Steps(pool, C["pool"])
            own.step(pool.memset(xg[:, :], 0.0))
            own.step(pool.iota(io32[:, :], [[1, P]], base=0, channel_multiplier=0))
            own.step(pool.tensor_copy(iota[:, :], io32[:, :]))
            own.step(pool.iota(toki[:, :], [[P, 3]], base=0, channel_multiplier=1))
            own.step(pool.tensor_copy(tok[:, :], toki[:, :]))
            own.step(pool.tensor_scalar(valid[:, :], tok[:, :], float(T), None, ALU.is_lt))
            own.step(pool.tensor_scalar(tokc[:, :], tok[:, :], -1.0, float(T), ALU.mult, ALU.add))
            own.step(pool.memset(manyf[:, :], 1.0))
            own.step(pool.iota(io32[:, :].rearrange("p (h b s) -> p h b s", h=2, b=2), [[HALF, 2], [SLOTS, 2], [1, HALF]],
                               base=0, channel_multiplier=0))
            own.step(pool.tensor_copy(slot_of[:, :], io32[:, :]))
            own.step(pool.iota(io32[:, :].rearrange("p (h d s) -> p h d s", h=2, d=2), [[HALF, 2], [0, 2], [1, HALF]],
                               base=0, channel_multiplier=0))
            own.step(pool.tensor_copy(slot2_of[:, :], io32[:, :]))
            for k in range(2):
                own.step(pool.tensor_scalar(destc[:, :, k], tok[:, :], -2.0, float(4 * T - 2 * T * k), ALU.mult, ALU.add))
                own.step(pool.tensor_tensor(destc[:, :, k], destc[:, :, k], valid[:, :], ALU.mult))
            for i in range(3):
                own.step(pool.tensor_scalar(dtmp[:, i:i + 1], tok[:, 0:1], float(HALF * (i + 1)), None, ALU.is_ge))
            own.step(pool.tensor_tensor(dtmp[:, 0:1], dtmp[:, 0:1], dtmp[:, 1:2], ALU.subtract))
            own.step(pool.tensor_tensor(dtmp[:, 0:1], dtmp[:, 0:1], dtmp[:, 2:3], ALU.add))
            own.step(pool.tensor_scalar(drow[:, :], dtmp[:, 0:1], float(4 * T), None, ALU.add))
            own.step(pool.tensor_scalar(thr[:, :], iota[:, 0:4], float(SLOTS), float(SLOTS), ALU.mult, ALU.add))
            pool.memset(lg[:, :, :], 0.0).then_inc(C["iota"], 1)

        @block.tensor
        def _(pe):
            def column_sums(out, src, c0, n, done):
                for c in range(n):
                    mm = pe.matmul(out, ones[:, :], src[:, c0 + c, :], start=(c == 0), stop=(c == n - 1))
                mm.then_inc(C[done], 1)

            pe.wait_ge(C["sq"], 1)
            column_sums(bank[0][:, 0:T], xn, 0, H, "ss")
            column_sums(bank[1][:, 0:T], xn, H, H, "ss")
            pe.wait_ge(C["on"], 2 * H)
            with pe.Fori(0, 2) as r:
                for j in range(4):
                    pe.wait_ge(W[j], 16 * r + 16)
                    for m in range(2):
                        for c in range(KC):
                            mm = pe.matmul(bank[2 * j + m][:, 0:T], ws[:, j, c * 256 + m * P:c * 256 + (m + 1) * P],
                                           qo[:, c, :], start=(c == 0), stop=(c == KC - 1))
                        mm.then_inc(C["o_done"], 1)
                pe.wait_ge(C["h"], 8 * r + 8)
            pe.wait_ge(C["sq2"], KC)
            column_sums(bank[0][:, 0:T], qo, 0, KC, "ss2")
            for c in range(KC):
                pe.wait_ge(C["un"], c + 1)
                r0 = c % 2 * 64
                mm = pe.matmul(bank[1][r0:r0 + 64, 0:T], wr[:, c, :], xn[:, c, :], start=(c < 2), stop=(c >= KC - 2))
            mm.then_inc(C["lp"], 1)
            for i in range(12):
                if i == 4:
                    pe.wait_ge(C["lpc"], 2)
                    for t, (lo, n) in enumerate(TILES):
                        mm = pe.matmul(bank[2][0:n, t * 64:t * 64 + NG + NE], lpart[:, lo:lo + n], fold[:, :], start=True, stop=True)
                    mm.then_inc(C["lgp"], 1)
                lo, n = TILES[i // 4]
                if i >= 4:
                    pe.wait_ge(C["rcopy"], i - 3)
                for c in range(4):
                    mm = pe.transpose(bank[4 + i % 4][0:n, c * P:(c + 1) * P], xn[:, 4 * (i % 4) + c, lo:lo + n], ident[:, :])
                mm.then_inc(C["rt"], 1)
            pe.wait_ge(C["mask"], 1)
            for t in range(3):
                out = bank[2][:, t * NE:(t + 1) * NE]
                for s in range(t):
                    pe.matmul(out, ones[:, :], mask[:, s, :], start=(s == 0), stop=False)
                mm = pe.matmul(out, tri_lt[:, :], mask[:, t, :], start=(t == 0), stop=True)
            for t in range(3):
                pe.matmul(bank[3][0:NE, 0:P], mask[:, t, :], ones[:, :], start=(t == 0), stop=(t == 2))
            for t in range(3):
                mm = pe.matmul(bank[2][:, 3 * NE:4 * NE], ones[:, :], mask[:, t, :], start=(t == 0), stop=(t == 2))
            mm.then_inc(C["cnt"], 1)
            pe.wait_ge(C["ex"], 1)
            pe.matmul(bank[3][:, P:P + NE], ext[:, :], tri_lt[0:NE, 0:NE], start=True, stop=True)
            pe.matmul(bank[3][:, P + NE:P + 2 * NE], ext[:, :], ident[0:NE, 0:NE], start=True, stop=True).then_inc(C["pe2"], 1)
            pe.wait_ge(C["oh"], 1)
            for i in range(6):
                pe.matmul(bank[0][:, 0:PAIRS], ohs[:, i // 2, i % 2, :], ohb[:, i // 2, i % 2, :],
                          start=(i == 0), stop=(i == 5))
            pe.wait_ge(C["oh"], 2)
            for i in range(6):
                mm = pe.matmul(bank[0][:, PAIRS:PAIRS + BLOCKS], ohs2[:, i // 2, i % 2, :], ohb2[:, i // 2, i % 2, :],
                               start=(i == 0), stop=(i == 5))
            mm.then_inc(C["idxp"], 1)

        @block.scalar
        def _(act):
            act.wait_ge(C["gg"], 1)
            nc.scalar.activation(xn[:, :, :].rearrange("p c t -> p (c t)"), qo[:, :, :].rearrange("p c t -> p (c t)"),
                                 ACT.Square).then_inc(C["sq"], 1)
            act.wait_ge(C["ms"], 2)
            nc.scalar.activation(rst[:, :, :], rst[:, :, :], ACT.Sqrt).then_inc(C["sqrt"], 1)
            act.wait_ge(C["o_done"], KC)
            for c in range(KC):
                act.wait_ge(C["h"], c + 1)
                nc.scalar.activation(qo[:, c, :], xT[:, c, :], ACT.Square).then_inc(C["sq2"], 1)
            act.wait_ge(C["ms2"], 1)
            nc.scalar.activation(rst[:, 0, :], rst[:, 0, :], ACT.Sqrt).then_inc(C["sqrt2"], 1)
            for i in range(12):
                t, k = i // 4, i % 4
                lo, n = TILES[t]
                if i == 8:
                    act.wait_ge(C["rst0"], 16)
                act.wait_ge(C["rt"], i + 1)
                nc.scalar.activation(stage[0:n, t % 2, k * 512:(k + 1) * 512], bank[4 + k][0:n, :], ACT.Copy).then_inc(C["rcopy"], 1)
                if k == 3:
                    act.wait_ge(C["rcopy"], i + 1)
                    act.dma_start(u_rows[lo:lo + n, :], stage[0:n, t % 2, :]).then_inc(C[f"rst{t % 2}"], 16)
            act.wait_ge(C["act"], 1)
            nc.scalar.activation(r2[:, :, :], r2[:, :, :], ACT.Exp).then_inc(C["gg"], 1)
            act.wait_ge(C["rst0"], 32)
            act.wait_ge(C["rst1"], 16)

        @block.vector
        def _(dve):
            own = Steps(dve, C["dve"])
            nc.vector.memset(r2[:, :, :], 0.0).then_inc(C["gg"], 1)
            dve.wait_ge(C["ss"], 2)
            for g in range(2):
                mean_square(dve, g, bank[g][:, 0:T], H * HD, "ms")
            dve.wait_ge(C["sqrt"], 1)
            own.step(dve.reciprocal(rstd[:, :, :], rst[:, :, :]))
            for c in range(2 * H):
                dve.scalar_tensor_tensor(out=qo[:, c, :], in0=qo[:, c, :], scalar=gcol[:, G_GRP + c:G_GRP + c + 1],
                                         in1=rstd[:, c // H, :], op0=ALU.mult, op1=ALU.mult).then_inc(C["on"], 1)
            with dve.Fori(0, 2) as r:
                for i in range(8):
                    dve.wait_ge(C["o_done"], 8 * r + i + 1)
                    dve.tensor_tensor(at(xT, 8 * r + i, 0, T), at(xT, 8 * r + i, 0, T), bank[i][:, 0:T],
                                      ALU.add).then_inc(C["h"], 1)
            dve.wait_ge(C["ss2"], 1)
            mean_square(dve, 0, bank[0][:, 0:T], D, "ms2")
            dve.wait_ge(C["sqrt2"], 1)
            own.step(dve.reciprocal(rstd[:, 0, :], rst[:, 0, :]))
            for c in range(KC):
                dve.scalar_tensor_tensor(out=xn[:, c, :], in0=xT[:, c, :], scalar=gcol[:, G_FFN + c:G_FFN + c + 1],
                                         in1=rstd[:, 0, :], op0=ALU.mult, op1=ALU.mult).then_inc(C["un"], 1)
            dve.tensor_tensor(fold[:, :], ident[:, 0:NG + NE], ident[:, 64:64 + NG + NE], ALU.add).then_inc(C["lpc"], 1)
            dve.wait_ge(C["lp"], 1)
            dve.tensor_copy(lpart[:, :], bank[1][:, 0:T]).then_inc(C["lpc"], 1)
            dve.wait_ge(C["iota"], 1)
            dve.wait_ge(C["lgp"], 1)

            def tt(out, x, y, op):
                own.step(dve.tensor_tensor(out, x, y, op))

            def ts(out, x, s1, s2, op0, op1=ALU.bypass):
                own.step(dve.tensor_scalar(out, x, s1, s2, op0, op1) if s2 is not None else dve.tensor_scalar(out, x, s1, None, op0))

            def red(out, x, op):
                own.step(dve.tensor_reduce(out, x, AX, op))

            for t, (lo, n) in enumerate(TILES):
                tt(lg[0:n, t, :], bank[2][0:n, t * 64:t * 64 + NG + NE], br[0:n, :], ALU.add)
            iota4 = iota[:, 0:NG].rearrange("p (t e) -> p t e", t=1).to_broadcast([P, 3, NG])
            iota32 = iota[:, 0:NE].rearrange("p (t e) -> p t e", t=1).to_broadcast([P, 3, NE])

            def first_max(x, n, numbers, best, hot, scratch, number):
                red(best, x, ALU.max)
                tt(scratch, x, over(best, n), ALU.is_lt)
                ts(scratch, scratch, 1.0e4, None, ALU.mult)
                tt(scratch, scratch, numbers, ALU.add)
                red(number, scratch, ALU.min)
                tt(hot, numbers, over(number, n), ALU.is_equal)

            first_max(lg[:, :, 0:NG], NG, iota4, gmx[:, :], gsel[:, :, :], rg[:, :, :], top[0][:, :])
            tt(r2[:, :, 0:NG], lg[:, :, 0:NG], over(gmx[:, :], NG), ALU.subtract)
            ts(re_[:, :, :].rearrange("p t (g e) -> p (t g) e", g=NG),
               over(gsel[:, :, :].rearrange("p t g -> p (t g)"), EPG), -1.0, ROUTE_BIG, ALU.add, ALU.mult)
            tt(re_[:, :, :], re_[:, :, :], lg[:, :, NG:NG + NE], ALU.add)
            first_max(re_[:, :, :], NE, iota32, top[0][:, :], oh[0][:, :, :], tmp[:, :, :], eid[:, :, 0])
            ts(tmp[:, :, :], oh[0][:, :, :], -2.0 * ROUTE_BIG, None, ALU.mult)
            tt(re_[:, :, :], re_[:, :, :], tmp[:, :, :], ALU.add)
            first_max(re_[:, :, :], NE, iota32, top[1][:, :], oh[1][:, :, :], tmp[:, :, :], eid[:, :, 1])
            dve.tensor_tensor(r2[:, :, NG], top[1][:, :], top[0][:, :], ALU.subtract).then_inc(C["act"], 1)
            tt(mask[:, :, :], oh[0][:, :, :], oh[1][:, :, :], ALU.add)
            dve.tensor_tensor(mask[:, :, :], mask[:, :, :], over(valid[:, :], NE), ALU.mult).then_inc(C["mask"], 1)
            dve.wait_ge(C["cnt"], 1)
            ts(manyf[:, 0:NE], bank[2][0:1, 3 * NE:4 * NE], float(HALF), None, ALU.is_gt)
            own.step(dve.tensor_copy(many[:, :], manyf[:, :]))
            red(many2[:, :], manyf[:, :].rearrange("p (n b) -> p n b", b=2), ALU.max)
            for j in range(4):
                ts(cnt4[:, j, :], bank[3][0:NE, 0:P], float(SLOTS * (j + 1)), None, ALU.is_gt)
            own.step(dve.tensor_reduce(ext[:, :], cnt4[:, :, :].rearrange("e j p -> e p j"), AX, ALU.add))
            dve.tensor_copy(rks[:, :, :].rearrange("p t e -> p (t e)"), bank[2][:, 0:3 * NE]).then_inc(C["ex"], 1)
            dve.wait_ge(C["pe2"], 1)
            own.step(dve.tensor_copy(base[:, :, :].rearrange("p a e -> p (a e)"), bank[3][:, P:P + 2 * NE]))
            b0 = base[:, 0, :].rearrange("p (t e) -> p t e", t=1).to_broadcast([P, 3, NE])
            for k in range(2):
                tt(tmp[:, :, :], oh[k][:, :, :], rks[:, :, :], ALU.mult)
                red(rank[:, :, k], tmp[:, :, :], ALU.add)
                tt(tmp[:, :, :], oh[k][:, :, :], b0, ALU.mult)
                red(pre[:, :, k], tmp[:, :, :], ALU.add)
            flat = lambda x: x.rearrange("p t k -> p (t k)")
            tt(cmp6[:, :, :, :].rearrange("p t k j -> p (t k) j"), over(flat(rank[:, :, :]), 4),
               thr[:, :].rearrange("p (a j) -> p a j", a=1).to_broadcast([P, 6, 4]), ALU.is_ge)
            red(flat(full[:, :, :]), cmp6[:, :, :, :].rearrange("p t k j -> p (t k) j"), ALU.add)
            ts(flat(first[:, :, :]), flat(full[:, :, :]), 0.0, None, ALU.is_equal)
            tt(flat(blk[:, :, :]), flat(pre[:, :, :]), flat(full[:, :, :]), ALU.add)
            ts(flat(blk[:, :, :]), flat(blk[:, :, :]), float(NE - 1), None, ALU.add)
            tt(flat(small[:, :, :]), flat(eid[:, :, :]), flat(blk[:, :, :]), ALU.subtract)
            tt(flat(small[:, :, :]), flat(small[:, :, :]), flat(first[:, :, :]), ALU.mult)
            tt(flat(blk[:, :, :]), flat(blk[:, :, :]), flat(small[:, :, :]), ALU.add)
            ts(flat(in_blk[:, :, :]), flat(full[:, :, :]), -float(SLOTS), None, ALU.mult)
            tt(flat(in_blk[:, :, :]), flat(in_blk[:, :, :]), flat(rank[:, :, :]), ALU.add)
            to_block = ohb2[:, :, :, :].rearrange("p t k b -> p (t k) b")
            tt(to_block, over(flat(blk[:, :, :]), BLOCKS),
               iota[:, 0:BLOCKS].rearrange("p (a b) -> p a b", a=1).to_broadcast([P, 6, BLOCKS]), ALU.is_equal)
            by_pair = to_block.rearrange("p a (n b) -> p (a n) b", b=2)
            ohbv = ohb[:, :, :, :].rearrange("p t k n -> p (t k n)")
            red(ohbv, by_pair, ALU.add)
            red(flat(odd[:, :, :]), to_block.rearrange("p a (n b) -> p b a n", b=2)[:, 1, :, :], ALU.add)
            ts(flat(odd[:, :, :]), flat(odd[:, :, :]), float(SLOTS), None, ALU.mult)
            tt(flat(odd[:, :, :]), flat(odd[:, :, :]), flat(in_blk[:, :, :]), ALU.add)
            for t in range(3):
                ts(ohb[:, t, :, :], ohb[:, t, :, :], tokc[:, t:t + 1], valid[:, t:t + 1], ALU.mult, ALU.mult)
            dve.tensor_tensor(ohs[:, :, :, :].rearrange("p t k s -> p (t k) s"), over(flat(odd[:, :, :]), P),
                              slot_of[:, :].rearrange("p (a s) -> p a s", a=1).to_broadcast([P, 6, P]),
                              ALU.is_equal).then_inc(C["oh"], 1)
            tt(to_block, to_block, over(flat(destc[:, :, :]), BLOCKS), ALU.mult)
            dve.tensor_tensor(ohs2[:, :, :, :].rearrange("p t k s -> p (t k) s"), over(flat(in_blk[:, :, :]), P),
                              slot2_of[:, :].rearrange("p (a s) -> p a s", a=1).to_broadcast([P, 6, P]),
                              ALU.is_equal).then_inc(C["oh"], 1)
            io8 = iota[0:1, 0:EXTRA].rearrange("p (b e) -> p b e", e=1).to_broadcast([1, EXTRA, NE])
            be = base[0:1, 0, :].rearrange("p (b e) -> p b e", b=1).to_broadcast([1, EXTRA, NE])
            ce = base[0:1, 1, :].rearrange("p (b e) -> p b e", b=1).to_broadcast([1, EXTRA, NE])
            tt(xb[:, :, :], io8, be, ALU.subtract)
            tt(xb2[:, :, :], xb[:, :, :], ce, ALU.is_lt)
            ts(xb[:, :, :], xb[:, :, :], 0.0, None, ALU.is_ge)
            tt(xb[:, :, :], xb[:, :, :], xb2[:, :, :], ALU.mult)
            red(xo[:, 1, :], xb[:, :, :], ALU.add)
            tt(xb[:, :, :], xb[:, :, :], iota[0:1, 0:NE].rearrange("p (b e) -> p b e", b=1).to_broadcast([1, EXTRA, NE]), ALU.mult)
            red(xo[:, 0, :], xb[:, :, :], ALU.add)
            own.step(dve.tensor_copy(extra[:, :, :], xo[:, :, :]))
            dve.wait_ge(C["gg"], 2)
            red(gmx[:, :], r2[:, :, 0:NG], ALU.add)
            own.step(dve.reciprocal(gmx[:, :], gmx[:, :]))
            ts(top[0][:, :], r2[:, :, NG], 1.0, None, ALU.add)
            own.step(dve.reciprocal(top[0][:, :], top[0][:, :]))
            tt(gates[:, :, 0], top[0][:, :], gmx[:, :], ALU.mult)
            tt(gates[:, :, 1], gates[:, :, 0], r2[:, :, NG], ALU.mult)
            dve.wait_ge(C["idxp"], 1)
            own.step(dve.tensor_scalar(idx[:, :], bank[0][:, 0:PAIRS], -1.0, float(T), ALU.mult, ALU.add))
            own.step(dve.tensor_scalar(dest[:, :], bank[0][:, PAIRS:PAIRS + BLOCKS], -1.0, drow[:, 0:1], ALU.mult, ALU.add))
    cctx.close()
    done_with(nc, C)

    gf = sb("gf", [P, D])
    dctx = ExitStack()
    xgT = sb("xgT", [P, KC, P], where=dctx)
    gu = [sb(f"gu{k}", [P, 256], where=dctx) for k in range(2)]
    si = [sb(f"si{k}", [P, 2, SLOTS], where=dctx) for k in range(2)]
    hT = [sb(f"hT{k}", [P, 2, SLOTS], where=dctx) for k in range(2)]
    ys = [sb(f"ys{k}", [P, 1024], where=dctx) for k in range(2)]
    pad = sb("pad", [1, 8], where=dctx)
    E = {n: sem("d_" + n) for n in (
        "xg xgp xgT gu0 gu1 guc0 guc1 t0 t1 si0 si1 h0 h1 y0 y1 yc0 yc1 yst0 yst1 pad gf").split()}
    y_half = y_rows.rearrange("r (c d) -> (r c) d", c=2)
    EXP_PAIRS = NE // 2

    def in_use(eng, i):
        return eng.value_load(extra[0:1, 1, bass.ds(i, 1)], min_val=0, max_val=1)

    def extra_pairs(eng, pair):
        with eng.If(in_use(eng, 0) > 0):
            with eng.Fori(EXP_PAIRS, PAIRS) as n:
                with eng.If(in_use(eng, 2 * (n - EXP_PAIRS)) > 0):
                    pair(n)

    with nc.Block() as block:
        @block.sync
        def _(sp):
            def free(k, n):
                sp.wait_ge(E[f"gu{k // 3}"] if k % 3 < 2 else E[f"y{k // 3}"], n)

            with sp.Fori(1, EXP_PAIRS) as n:
                for k in range(6):
                    free(k, n)
                    load_expert(sp, a, ws, W, k, 2 * n + k // 3)

            def pair(n):
                for blk_ in range(2):
                    e = sp.value_load(extra[0:1, 0, bass.ds((n - EXP_PAIRS) * 2 + blk_, 1)], min_val=0, max_val=NE - 1)
                    for k in range(3 * blk_, 3 * blk_ + 3):
                        free(k, n)
                        load_expert(sp, a, ws, W, k, e)

            extra_pairs(sp, pair)

        @block.gpsimd
        def _(pool):
            def gather(n, rows):
                pool.indirect_dma_start(xg[0:rows, :], None, u_rows,
                                        bass.IndirectOffsetOnAxis(ap=idx[0:rows, n:n + 1], axis=0),
                                        bounds_check=T - 1, oob_is_err=False).then_inc(E["xg"], 16)

            def tokens(n):
                rest = pool.value_load(many2[0:1, n:n + 1], min_val=0, max_val=1)
                wait_past(pool, E["xgp"], 4 * n)
                with pool.If(rest > 0):
                    gather(n, P)
                with pool.Else():
                    gather(n, SLOTS)

            def scatter(n, k, rows):
                pool.indirect_dma_start(y_half, bass.IndirectOffsetOnAxis(ap=dest[0:rows, 2 * n + k:2 * n + k + 1], axis=0),
                                        ys[k][0:rows, :], None,
                                        bounds_check=4 * T - 1, oob_is_err=False).then_inc(E[f"yst{k}"], 16)

            def store(n):
                for k in range(2):
                    rest = pool.value_load(many[0:1, 2 * n + k:2 * n + k + 1], min_val=0, max_val=1)
                    pool.wait_ge(E[f"yc{k}"], 2 * n + 2)
                    with pool.If(rest > 0):
                        scatter(n, k, P)
                    with pool.Else():
                        scatter(n, k, SLOTS)

            tokens(0)
            tokens(1)
            for n in range(EXP_PAIRS):
                if n + 2 < EXP_PAIRS:
                    tokens(n + 2)
                store(n)
            for k in range(2):
                pool.wait_ge(E[f"yst{k}"], 16 * EXP_PAIRS)
            pool.memset(pad[:, 0:1], 0.0).then_inc(E["pad"], 1)
            for n in range(EXP_PAIRS, PAIRS):
                with pool.If(in_use(pool, 2 * (n - EXP_PAIRS)) > 0):
                    tokens(n)
                    store(n)
                    for k in range(2):
                        pool.wait_ge(E[f"yst{k}"], 16 * n + 16)
                    pool.memset(pad[:, n - EXP_PAIRS + 1:n - EXP_PAIRS + 2], 0.0).then_inc(E["pad"], 1)

        @block.tensor
        def _(pe):
            def tokens(n, stored):
                pe.wait_ge(E["xg"], 16 * n + 16)
                wait_past(pe, E["yc0"], 2 * stored)
                wait_past(pe, E["yc1"], 2 * stored)
                xv = xg[:, :].rearrange("s (p c) -> s c p", c=KC)
                for k in range(4):
                    for c in range(4):
                        out = bank[4 + k][:, c * P:(c + 1) * P].rearrange("p (b h s) -> p h b s", b=2, h=2)
                        mm = pe.transpose(out, xv[:, 4 * k + c, :], ident[:, :])
                    mm.then_inc(E["xgp"], 1)

            def gate_up(k, n):
                wg, wu = SLOT[3 * k], SLOT[3 * k + 1]
                pe.wait_ge(W[wg], 16 * (n + FIRST[wg]))
                pe.wait_ge(W[wu], 16 * (n + FIRST[wu]))
                for c in range(KC):
                    lhs = xgT[:, c, k * SLOTS:(k + 1) * SLOTS]
                    pe.matmul(bank[2 * k][0:SLOTS, 0:256], lhs, ws[:, wg, c * 256:(c + 1) * 256],
                              start=(c == 0), stop=(c == KC - 1))
                    mm = pe.matmul(bank[2 * k][SLOTS:P, 0:256], lhs, ws[:, wu, c * 256:(c + 1) * 256],
                                   start=(c == 0), stop=(c == KC - 1))
                mm.then_inc(E[f"gu{k}"], 1)

            def turn_over(k, n):
                pe.wait_ge(E[f"guc{k}"], n + 1)
                for j in range(2):
                    mm = pe.transpose(bank[2 * k + 1][:, j * P:(j + 1) * P], gu[k][:, j * P:(j + 1) * P], ident[:, :])
                mm.then_inc(E[f"t{k}"], 1)

            def down(k, n):
                wd = SLOT[3 * k + 2]
                pe.wait_ge(W[wd], 16 * (n + FIRST[wd]))
                pe.wait_ge(E[f"h{k}"], n + 1)
                for dc in range(2):
                    for j in range(2):
                        for q in range(4):
                            h0, d0 = q // 2 * HALF, j * D + q % 2 * 1024 + dc * 512
                            mm = pe.matmul(bank[4 + 2 * k + dc][q * HALF:(q + 1) * HALF, :], hT[k][:, j, h0:h0 + HALF],
                                           ws[:, wd, d0:d0 + 512], start=(j == 0), stop=(j == 1))
                mm.then_inc(E[f"y{k}"], 1)

            def pair(n, ahead):
                pe.wait_ge(E["xgT"], 4 * n + 4)
                gate_up(0, n)
                gate_up(1, n)
                turn_over(0, n)
                if ahead:
                    tokens(n + 1, n)
                turn_over(1, n)
                if ahead:
                    pe.wait_ge(E["xgT"], 4 * n + 8)
                down(0, n)
                down(1, n)

            def lone_pair(n):
                tokens(n, n)
                pair(n, False)

            tokens(0, 0)
            pair(0, True)
            with pe.Fori(1, EXP_PAIRS - 1) as n:
                pair(n, True)
            pair(EXP_PAIRS - 1, False)
            extra_pairs(pe, lone_pair)

        @block.scalar
        def _(act):
            def tokens(n):
                wait_past(act, E["gu1"], n)
                for k in range(4):
                    act.wait_ge(E["xgp"], 4 * n + k + 1)
                    nc.scalar.activation(xgT[:, 4 * k:4 * k + 4, :].rearrange("p c s -> p (c s)"), bank[4 + k][:, :],
                                         ACT.Copy).then_inc(E["xgT"], 1)

            def silu(k, n):
                act.wait_ge(E[f"t{k}"], n + 1)
                wait_past(act, E[f"h{k}"], n)
                gv = bank[2 * k + 1][:, 0:256].rearrange("p (j s) -> p j s", j=2)
                nc.scalar.activation(si[k][:, :, :], gv[:, :, 0:SLOTS], ACT.Silu).then_inc(E[f"si{k}"], 1)

            def pair(n, ahead):
                silu(0, n)
                if ahead:
                    tokens(n + 1)
                silu(1, n)
                act.wait_ge(E["y1"], n + 1)
                wait_past(act, E["yst1"], 16 * n)
                for i in range(2):
                    nc.scalar.activation(ys[1][:, i * 512:(i + 1) * 512], bank[6 + i][:, :], ACT.Copy).then_inc(E["yc1"], 1)

            def lone_pair(n):
                tokens(n)
                pair(n, False)

            act.dma_start(gf[:, :], a["norm_final_g"].rearrange("(a d) -> a d", a=1).to_broadcast([P, D])).then_inc(E["gf"], 16)
            tokens(0)
            pair(0, True)
            with act.Fori(1, EXP_PAIRS - 1) as n:
                pair(n, True)
            pair(EXP_PAIRS - 1, False)
            extra_pairs(act, lone_pair)

        @block.vector
        def _(dve):
            def pair(n):
                for k in range(2):
                    dve.wait_ge(E[f"gu{k}"], n + 1)
                    wait_past(dve, E[f"t{k}"], n)
                    dve.tensor_copy(gu[k][:, :], bank[2 * k][:, 0:256]).then_inc(E[f"guc{k}"], 1)
                for k in range(2):
                    dve.wait_ge(E[f"si{k}"], n + 1)
                    wait_past(dve, E[f"y{k}"], n)
                    uv = bank[2 * k + 1][:, 0:256].rearrange("p (j s) -> p j s", j=2)
                    dve.tensor_tensor(hT[k][:, :, :], si[k][:, :, :], uv[:, :, SLOTS:P], ALU.mult).then_inc(E[f"h{k}"], 1)
                dve.wait_ge(E["y0"], n + 1)
                wait_past(dve, E["yst0"], 16 * n)
                for i in range(2):
                    dve.tensor_copy(ys[0][:, i * 512:(i + 1) * 512], bank[4 + i][:, :]).then_inc(E["yc0"], 1)

            pair(0)
            with dve.Fori(1, EXP_PAIRS) as n:
                pair(n)
            extra_pairs(dve, pair)
    dctx.close()

    ORDER = [2, 0, 1]
    with ExitStack() as ectx:
        rows = ws[:, :, :].rearrange("p s (a d) -> p (s a) d", d=D)
        hr = rows[:, 0:3, :]
        yr = rows[:, 3:9, :].rearrange("p (t k) d -> p t k d", k=2)
        junk = rows[:, 9, :]
        ssq = sb("ssq", [P, 3], where=ectx)
        rms = sb("rms", [P, 3], where=ectx)
        F = {n: sem("e_" + n) for n in "hp half g20 g21 g00 g01 g10 g11 sum sq ms sqrt out st dve".split()}
        with nc.Block() as block:
            @block.sync
            def _(sp):
                for t in ORDER:
                    lo, n = TILES[t]
                    for k in range(2):
                        sp.dma_start(yr[0:n, t, k, :], y_rows[k * T + lo:k * T + lo + n, :]).then_inc(F[f"g{t}{k}"], 16)
                for i, t in enumerate(ORDER):
                    lo, n = TILES[t]
                    sp.wait_ge(F["out"], i + 1)
                    dst = y_prompt[0, lo:lo + n] if t < 2 else y_sample.rearrange("b s d -> (b s) d")
                    sp.dma_start(dst, hr[0:n, t, :]).then_inc(F["st"], 16)
                sp.wait_ge(F["st"], 48)

            @block.tensor
            def _(pe):
                for i in range(12):
                    lo, n = TILES[ORDER[i // 4]]
                    if i >= 8:
                        pe.wait_ge(F["half"], i - 7)
                    for c in range(4):
                        mm = pe.transpose(bank[i % 8][0:n, c * P:(c + 1) * P], xT[:, 4 * (i % 4) + c, lo:lo + n], ident[:, :])
                    mm.then_inc(F["hp"], 1)

            @block.scalar
            def _(act):
                for i, t in enumerate(ORDER):
                    n = TILES[t][1]
                    act.wait_ge(F["sum"], i + 1)
                    if i:
                        act.wait_ge(F["sq"], i)
                    nc.scalar.activation(junk[0:n, :], hr[0:n, t, :], ACT.Square, accum_out=ssq[0:n, t:t + 1]).then_inc(F["sq"], 1)
                    act.wait_ge(F["ms"], i + 1)
                    nc.scalar.activation(rms[0:n, t:t + 1], rms[0:n, t:t + 1], ACT.Sqrt).then_inc(F["sqrt"], 1)

            @block.vector
            def _(dve):
                own = Steps(dve, F["dve"])

                def add(i):
                    t = ORDER[i]
                    n = TILES[t][1]
                    dve.wait_ge(F[f"g{t}0"], 16)
                    for k in range(4):
                        dve.wait_ge(F["hp"], 4 * i + k + 1)
                        col = slice(k * 512, (k + 1) * 512)
                        dve.scalar_tensor_tensor(out=hr[0:n, t, col], in0=yr[0:n, t, 0, col], scalar=gates[0:n, t, 0:1],
                                                 in1=bank[(4 * i + k) % 8][0:n, :], op0=ALU.mult, op1=ALU.add).then_inc(F["half"], 1)
                    dve.wait_ge(F["half"], 4 * i + 4)
                    dve.wait_ge(F[f"g{t}1"], 16)
                    dve.scalar_tensor_tensor(out=hr[0:n, t, :], in0=yr[0:n, t, 1, :], scalar=gates[0:n, t, 1:2],
                                             in1=hr[0:n, t, :], op0=ALU.mult, op1=ALU.add).then_inc(F["sum"], 1)

                def norm(i):
                    t = ORDER[i]
                    n = TILES[t][1]
                    dve.wait_ge(F["sq"], i + 1)
                    dve.tensor_scalar(rms[0:n, t:t + 1], ssq[0:n, t:t + 1], 1.0 / D, EPS, ALU.mult, ALU.add).then_inc(F["ms"], 1)
                    dve.wait_ge(F["sqrt"], i + 1)
                    own.step(dve.reciprocal(ssq[0:n, t:t + 1], rms[0:n, t:t + 1]))
                    if i == 0:
                        dve.wait_ge(E["gf"], 16)
                    dve.scalar_tensor_tensor(out=hr[0:n, t, :], in0=hr[0:n, t, :], scalar=ssq[0:n, t:t + 1],
                                             in1=gf[0:n, :], op0=ALU.mult, op1=ALU.mult).then_inc(F["out"], 1)

                add(0)
                add(1)
                norm(0)
                add(2)
                norm(1)
                norm(2)


_INS = ["x_prompt", "x_sample", "cache_sb_k", "cache_sb_v", "cache_fox_k", "cache_fox_v", "cache_fox_logf",
        "norm_attn_g", "w_in", "b_forget", "g_sb_out", "g_fox_out", "w_out", "norm_ffn_g", "w_router_group",
        "b_router_group", "w_router_expert", "b_router_expert", "w_expert_gate", "w_expert_up", "w_expert_down",
        "norm_final_g"]
_KV_P, _KV_S = (1, 1, SEQ, H, HD), (1, NB, 1, H, HD)
_OUTS = [(1, SEQ, D), (NB, 1, D), _KV_P, _KV_P, _KV_P, _KV_P, (1, 1, SEQ, H), _KV_S, _KV_S, _KV_S, _KV_S, (1, NB, 1, H)]


def kernel(**inputs):
    import numpy as _np
    import concourse.bacc as _bacc
    from concourse.bass_utils import run_bass_kernel_spmd as _run

    nc = _bacc.Bacc("TRN2", target_bir_lowering=False, num_devices=1)
    arrays, a = {}, {}
    data = {name: _np.ascontiguousarray(inputs[name]) for name in _INS}
    data["pages"] = _np.ascontiguousarray(inputs["page_table"][:, ::-1]).reshape(1, NB * PAGES)
    for name, x in data.items():
        arrays[f"in_{name}"] = x
        a[name] = nc.dram_tensor(f"in_{name}", x.shape, mybir.dt.from_np(x.dtype), kind="ExternalInput").ap()
    outs = [nc.dram_tensor(f"out_{i}", shape, F32, kind="ExternalOutput").ap() for i, shape in enumerate(_OUTS)]
    u_rows = nc.dram_tensor("u_rows", (T, D), F32).ap()
    y_rows = nc.dram_tensor("y_rows", (2 * T, D), F32).ap()
    hybrid_step(nc, a, outs, u_rows, y_rows)
    r = _run(nc, [arrays], core_ids=[0])
    return tuple(r.results[0][f"out_{i}"] for i in range(len(_OUTS)))
```
